# Optimizing a Trainium2 kernel written in Bass

```python
import math
import jax, jax.numpy as jnp
from jax import lax
import numpy as np

D_MODEL = 1024
BATCH = 1
SEQ = 512
DEPTH = 2

N_MIXERS = 2
N_META = 16
N_S5_LAYERS = (DEPTH + N_MIXERS - 1) // N_MIXERS
N_ATTN_LAYERS = DEPTH // N_MIXERS
S5_GROUP = 16
S5_GROUPS = D_MODEL // S5_GROUP
S5_STATE = 64
DT_MIN = 1e-3
DT_MAX = 1e-1
DA_HEADS = 8
DA_HEAD_DIM = D_MODEL // DA_HEADS // 2
DA_V_DIM = 2 * DA_HEAD_DIM
ROPE_THETA = 10000.0
Q_BLOCK = 128
D_FF = 256 * ((int(8 * D_MODEL / 3) + 255) // 256)
CONV_WIDTH = 3
EPS = 1e-6

kernel_name = "hybrid_s5_diffattn_convffn"

def rms_norm(x, gain):
    xf = x.astype(jnp.float32)
    y = xf * lax.rsqrt(jnp.mean(xf * xf, axis=-1, keepdims=True) + EPS)
    return (y * gain.astype(jnp.float32)).astype(x.dtype)

def _complex_linear_combine(left, right):
    a1r, a1i, b1r, b1i = left
    a2r, a2i, b2r, b2i = right
    ar = a2r * a1r - a2i * a1i
    ai = a2r * a1i + a2i * a1r
    br = a2r * b1r - a2i * b1i + b2r
    bi = a2r * b1i + a2i * b1r + b2i
    return ar, ai, br, bi

def s5_mixer(u, a_re, a_im, log_dt, b_re, b_im, c_re, c_im, d_skip, w_glu, b_glu):
    bsz, L, _ = u.shape
    f32 = jnp.float32
    dt = jnp.exp(log_dt.astype(f32))[:, None]
    lr = a_re.astype(f32)
    li = a_im.astype(f32)
    mag = jnp.exp(lr * dt)
    ab_re = mag * jnp.cos(li * dt)
    ab_im = mag * jnp.sin(li * dt)
    den = lr * lr + li * li
    n_re = ab_re - 1.0
    n_im = ab_im
    f_re = ((n_re * lr + n_im * li) / den)[..., None]
    f_im = ((n_im * lr - n_re * li) / den)[..., None]
    br = b_re.astype(f32)
    bi = b_im.astype(f32)
    bb_re = f_re * br - f_im * bi
    bb_im = f_re * bi + f_im * br
    ug = u.astype(f32).reshape(bsz, L, S5_GROUPS, S5_GROUP)
    bu_re = jnp.einsum('blgc,gnc->blgn', ug, bb_re)
    bu_im = jnp.einsum('blgc,gnc->blgn', ug, bb_im)
    a_seq_re = jnp.broadcast_to(ab_re, (1, L, S5_GROUPS, S5_STATE))
    a_seq_im = jnp.broadcast_to(ab_im, (1, L, S5_GROUPS, S5_STATE))
    _, _, s_re, s_im = lax.associative_scan(
        _complex_linear_combine, (a_seq_re, a_seq_im, bu_re, bu_im), axis=1)
    y = (jnp.einsum('blgn,gcn->blgc', s_re, c_re.astype(f32))
         - jnp.einsum('blgn,gcn->blgc', s_im, c_im.astype(f32)))
    y = y.reshape(bsz, L, D_MODEL) + d_skip.astype(f32) * u.astype(f32)
    z = jax.nn.gelu(y).astype(u.dtype)
    h = z @ w_glu + b_glu
    val, gate = jnp.split(h, 2, axis=-1)
    return val * jax.nn.sigmoid(gate)

def rope_tables(L):
    half = DA_HEAD_DIM // 2
    inv_freq = ROPE_THETA ** (-jnp.arange(half, dtype=jnp.float32) / half)
    ang = jnp.arange(L, dtype=jnp.float32)[:, None] * inv_freq[None, :]
    return jnp.cos(ang), jnp.sin(ang)

def apply_rope(x, cos, sin):
    x1, x2 = jnp.split(x.astype(jnp.float32), 2, axis=-1)
    c = cos[None, :, None, None, :]
    s = sin[None, :, None, None, :]
    return jnp.concatenate([x1 * c - x2 * s, x2 * c + x1 * s], axis=-1).astype(x.dtype)

def diff_attention(h, w_qkv, lam, subln_gain, w_o, lambda_init):
    bsz, L, _ = h.shape
    qkv = h @ w_qkv
    q, k, v = jnp.split(qkv, 3, axis=-1)
    q = q.reshape(bsz, L, DA_HEADS, 2, DA_HEAD_DIM)
    k = k.reshape(bsz, L, DA_HEADS, 2, DA_HEAD_DIM)
    v = v.reshape(bsz, L, DA_HEADS, DA_V_DIM)
    cos, sin = rope_tables(L)
    q = apply_rope(q, cos, sin)
    k = apply_rope(k, cos, sin)
    lamf = lam.astype(jnp.float32)
    lam_full = (jnp.exp(jnp.sum(lamf[0] * lamf[1])) - jnp.exp(jnp.sum(lamf[2] * lamf[3]))
                + lambda_init)
    n_blocks = -(-L // Q_BLOCK)
    L_pad = n_blocks * Q_BLOCK
    pad = L_pad - L
    q = jnp.pad(q, ((0, 0), (0, pad), (0, 0), (0, 0), (0, 0)))
    k = jnp.pad(k, ((0, 0), (0, pad), (0, 0), (0, 0), (0, 0)))
    v = jnp.pad(v, ((0, 0), (0, pad), (0, 0), (0, 0)))
    q_blocks = q.reshape(bsz, n_blocks, Q_BLOCK, DA_HEADS, 2, DA_HEAD_DIM).transpose(1, 0, 2, 3, 4, 5)
    key_pos = jnp.arange(L_pad)
    scale = DA_HEAD_DIM ** -0.5

    def one_block(args):
        qb, blk = args
        s = jnp.einsum('bqhcd,bkhcd->bhcqk', qb, k).astype(jnp.float32) * scale
        q_pos = blk * Q_BLOCK + jnp.arange(Q_BLOCK)
        mask = key_pos[None, :] <= q_pos[:, None]
        s = jnp.where(mask, s, -jnp.inf)
        p = jax.nn.softmax(s, axis=-1)
        attn = p[:, :, 0] - lam_full * p[:, :, 1]
        return jnp.einsum('bhqk,bkhe->bqhe', attn.astype(v.dtype), v)

    o = lax.map(one_block, (q_blocks, jnp.arange(n_blocks)))
    o = o.transpose(1, 0, 2, 3, 4).reshape(bsz, L_pad, DA_HEADS, DA_V_DIM)[:, :L]
    o = rms_norm(o, subln_gain) * (1.0 - lambda_init)
    return o.reshape(bsz, L, D_MODEL) @ w_o

def conv_ffn(h, w_up, conv_w, conv_b, w_down):
    L = h.shape[1]
    up = h @ w_up
    up_p = jnp.pad(up, ((0, 0), (CONV_WIDTH - 1, 0), (0, 0)))
    c = conv_b + sum(conv_w[j] * up_p[:, j:j + L] for j in range(CONV_WIDTH))
    gate, val = jnp.split(c, 2, axis=-1)
    return (jax.nn.silu(gate) * val) @ w_down

def setup_inputs(seed: int = 0) -> dict:
    key = jax.random.key(seed)
    ks = jax.random.split(key, 24)
    nrm = jax.random.normal
    G, N, C, D, F = S5_GROUPS, S5_STATE, S5_GROUP, D_MODEL, D_FF
    ns, na = N_S5_LAYERS, N_ATTN_LAYERS
    x = nrm(ks[0], (BATCH, SEQ, D), jnp.float32)
    meta_tokens = nrm(ks[1], (N_META, D), jnp.float32)
    norm_mix_gain = 1.0 + 0.02 * nrm(ks[2], (DEPTH, D), jnp.float32)
    norm_ffn_gain = 1.0 + 0.02 * nrm(ks[3], (DEPTH, D), jnp.float32)
    s5_a_re = -0.5 + 0.01 * nrm(ks[4], (ns, G, N), jnp.float32)
    s5_a_im = (jnp.pi * jnp.arange(N, dtype=jnp.float32))[None, None, :] + 0.01 * nrm(ks[5], (ns, G, N), jnp.float32)
    s5_log_dt = jax.random.uniform(ks[6], (ns, G), jnp.float32, math.log(DT_MIN), math.log(DT_MAX))
    s5_b_re = nrm(ks[7], (ns, G, N, C), jnp.float32) * (2 * C) ** -0.5
    s5_b_im = nrm(ks[8], (ns, G, N, C), jnp.float32) * (2 * C) ** -0.5
    s5_c_re = nrm(ks[9], (ns, G, C, N), jnp.float32) * N ** -0.5
    s5_c_im = nrm(ks[10], (ns, G, C, N), jnp.float32) * N ** -0.5
    s5_d = nrm(ks[11], (ns, D), jnp.float32)
    s5_w_glu = nrm(ks[12], (ns, D, 2 * D), jnp.float32) * D ** -0.5
    s5_b_glu = 0.01 * nrm(ks[13], (ns, 2 * D), jnp.float32)
    attn_w_qkv = nrm(ks[14], (na, D, 3 * D), jnp.float32) * D ** -0.5
    attn_lambda = 0.1 * nrm(ks[15], (na, 4, DA_HEAD_DIM), jnp.float32)
    attn_subln_gain = 1.0 + 0.02 * nrm(ks[16], (na, DA_V_DIM), jnp.float32)
    attn_w_o = nrm(ks[17], (na, D, D), jnp.float32) * D ** -0.5
    ffn_w_up = nrm(ks[18], (DEPTH, D, 2 * F), jnp.float32) * D ** -0.5
    ffn_conv_w = nrm(ks[19], (DEPTH, CONV_WIDTH, 2 * F), jnp.float32) * CONV_WIDTH ** -0.5
    ffn_conv_b = 0.01 * nrm(ks[20], (DEPTH, 2 * F), jnp.float32)
    ffn_w_down = nrm(ks[21], (DEPTH, F, D), jnp.float32) * F ** -0.5
    final_norm_gain = 1.0 + 0.02 * nrm(ks[22], (D,), jnp.float32)
    return {"x": x, "meta_tokens": meta_tokens, "norm_mix_gain": norm_mix_gain,
            "norm_ffn_gain": norm_ffn_gain, "s5_a_re": s5_a_re, "s5_a_im": s5_a_im,
            "s5_log_dt": s5_log_dt, "s5_b_re": s5_b_re, "s5_b_im": s5_b_im,
            "s5_c_re": s5_c_re, "s5_c_im": s5_c_im, "s5_d": s5_d, "s5_w_glu": s5_w_glu,
            "s5_b_glu": s5_b_glu, "attn_w_qkv": attn_w_qkv, "attn_lambda": attn_lambda,
            "attn_subln_gain": attn_subln_gain, "attn_w_o": attn_w_o, "ffn_w_up": ffn_w_up,
            "ffn_conv_w": ffn_conv_w, "ffn_conv_b": ffn_conv_b, "ffn_w_down": ffn_w_down,
            "final_norm_gain": final_norm_gain}

def reference(x, meta_tokens, norm_mix_gain, norm_ffn_gain, s5_a_re, s5_a_im, s5_log_dt,
              s5_b_re, s5_b_im, s5_c_re, s5_c_im, s5_d, s5_w_glu, s5_b_glu, attn_w_qkv,
              attn_lambda, attn_subln_gain, attn_w_o, ffn_w_up, ffn_conv_w, ffn_conv_b,
              ffn_w_down, final_norm_gain):
    bsz = x.shape[0]
    meta = jnp.broadcast_to(meta_tokens.astype(x.dtype)[None], (bsz, N_META, D_MODEL))
    h = jnp.concatenate([meta, x], axis=1)
    for i in range(DEPTH):
        j = i // N_MIXERS
        hn = rms_norm(h, norm_mix_gain[i])
        if i % N_MIXERS == 0:
            mix = s5_mixer(hn, s5_a_re[j], s5_a_im[j], s5_log_dt[j], s5_b_re[j], s5_b_im[j],
                           s5_c_re[j], s5_c_im[j], s5_d[j], s5_w_glu[j], s5_b_glu[j])
        else:
            lambda_init = 0.8 - 0.6 * math.exp(-0.3 * i)
            mix = diff_attention(hn, attn_w_qkv[j], attn_lambda[j], attn_subln_gain[j],
                                 attn_w_o[j], lambda_init)
        h = h + mix.astype(h.dtype)
        hn = rms_norm(h, norm_ffn_gain[i])
        h = h + conv_ffn(hn, ffn_w_up[i], ffn_conv_w[i], ffn_conv_b[i], ffn_w_down[i]).astype(h.dtype)
    out = rms_norm(h, final_norm_gain)
    return out[:, N_META:]


_drawn_inputs = setup_inputs


def setup_inputs(seed=0):
    import zlib

    import numpy as np

    out = dict(_drawn_inputs(seed))
    spreads = {}
    factors = {'norm_mix_gain': 2.952,
     'norm_ffn_gain': 2.986,
     's5_a_re': 8.0,
     's5_b_glu': 4.65,
     'attn_subln_gain': 5.399,
     'ffn_conv_b': 5.11,
     'final_norm_gain': 2.841}
    for name, (base, spread) in spreads.items():
        noise = np.random.default_rng([zlib.crc32(name.encode()), seed]).standard_normal(out[name].shape)
        drawn = base * np.exp(spread * noise) if base else spread * noise
        out[name] = __import__('jax').numpy.asarray(drawn.astype(out[name].dtype))
    for name, factor in factors.items():
        out[name] = (out[name] * factor).astype(out[name].dtype)
    return out
```

```python
import math
from contextlib import ExitStack

import numpy as np
import concourse.bass as bass
from concourse import mybir

F32 = mybir.dt.float32
F32R = mybir.dt.float32r
ACT = mybir.ActivationFunctionType
ALU = mybir.AluOpType
AX = mybir.AxisListType

P = 128
D = 1024
CT = D // P
META = 16
SEQ = 512
L = META + SEQ
FF = 2816
FT = FF // P
EPS = 1e-6
G, NST, GC = 64, 64, 16
T = 8
NK = L // T
BG = P // GC
HEADS, HD = 8, 64
LAMBDA_INIT = 0.8 - 0.6 * math.exp(-0.3 * 1)

CONV_W, CONV_B, GAIN_MIX, GAIN_FFN, B_GLU, SUBLN = 0, 264, 352, 368, 384, 400
PV_COLS = 401

U_GLU, U_UP0, U_DN0, U_QKV, U_WO, U_UP1, U_DN1, U_END = 0, 16, 60, 84, 108, 116, 160, 184

ALL = ((0, 264), (264, 264))
FROM12 = ((12, 258), (270, 258))
FROM16 = ((16, 256), (272, 256))

TILES = ((0, META),) + tuple((META + P * i, P) for i in range(SEQ // P))
NT = len(TILES)
CUT = META + 2 * P
PS_COL = 512 - CUT
SCALE = HD ** -0.5

WORDS0 = 16512
MAGIC = 1.5 * 2.0 ** 23
TWO_PI = 2.0 * math.pi
PI_A = 6.28125
PI_B = float(np.float32(round((TWO_PI - PI_A) * 2 ** 21) / 2 ** 21))
PI_C = float(np.float32(TWO_PI - PI_A - PI_B))
PI_MAX = 3.1415925


def shape_constants():
    eye = np.eye(P, dtype=np.float32)
    swap64 = np.roll(eye, 64, axis=0)
    swap32 = np.zeros((P, P), np.float32)
    for p in range(P):
        swap32[p ^ 32, p] = 1.0
    q, k = np.arange(P)[:, None], np.arange(P)[None, :]
    mask = np.where(k <= q, 0.0, -(2.0 ** 100)).astype(np.float32)
    sign = np.where(np.arange(P) < 64, 1.0, -1.0).astype(np.float32)[:, None]
    half = HD // 2
    inv = (10000.0 ** (-np.arange(half, dtype=np.float32) / np.float32(half))).astype(np.float32)
    ang = (np.arange(L, dtype=np.float32)[None, :] * inv[:, None]).astype(np.float32)
    cos = np.tile(np.cos(ang), (4, 1)).astype(np.float32)
    sin = np.tile(np.concatenate([-np.sin(ang), np.sin(ang)]), (2, 1)).astype(np.float32)
    return np.concatenate([eye, swap64, swap32, mask, sign, -sign, cos, sin], axis=1)


class Chain:

    def __init__(self, eng, sem):
        self.eng, self.sem, self.base, self.k = eng, sem, 0, 0

    def __call__(self, ins):
        ins.then_inc(self.sem, 1)
        self.k += 1
        self.eng.wait_ge(self.sem, self.base + self.k)

    def enter(self, i, steps):
        self.start, self.steps = self.base + self.k, steps
        self.base, self.k = i * steps + self.start, 0

    def leave(self, rounds):
        assert self.k == self.steps, (self.k, self.steps)
        self.base, self.k = self.start + rounds * self.steps, 0


def build(nc, inp, out):
    ds = bass.ds
    consts = nc.inline_tensor(shape_constants(), name="shape_constants").ap()
    ctx = ExitStack()
    with ctx:
        def sem(name):
            return ctx.enter_context(nc.semaphore(name))

        top = [0]

        def at(name, shape, dt, offset=None):
            words = int(np.prod(shape[1:]))
            o = top[0] if offset is None else offset
            if offset is None:
                top[0] += -(-words // 8) * 8
            return nc.alloc_sbuf_tensor_at(name, list(shape), dt, offset=WORDS0 + 4 * o)

        hT = at("hT", [P, CT, L], F32)
        O_HG = top[0]
        hgH = at("hgH", [P, CT, L], F32R)
        hgL = at("hgL", [P, CT, L], F32R)
        O_ACTH = top[0]
        actH = at("actH", [P, FT, L], F32R)
        O_ACTL = top[0]
        actL = at("actL", [P, FT, L], F32R)
        raw = at("raw", [P, 2, 8, P], F32)
        wH = at("wH", [P, 4, 8, P], F32R)
        O_WL = top[0]
        wL = at("wL", [P, 4, 8, P], F32R)
        O_WH = O_WL - 4096
        cst = at("cst", [P, 514], F32)
        PV = at("PV", [P, PV_COLS], F32)
        O_SCR = top[0]
        ones = at("ones", [P, P], F32)
        rstd = at("rstd", [P, L], F32)
        acc = at("acc", [P, L], F32)
        sqt = at("sqt", [P, L], F32)
        u = at("u", [P, 2, L + 2], F32)
        cg = at("cg", [P, L], F32)
        cv = at("cv", [P, L], F32)
        vstage = at("vstage", [P, 4, P], F32)
        tiny = at("tiny", [P, 640], F32)
        O_SPARE = top[0]
        cs = at("cs", [P, 2, L], F32, offset=O_SPARE)
        fgain = at("fgain", [P, D], F32, offset=O_SPARE)

        qk = at("qk", [P, 2 * HEADS, L], F32, offset=O_ACTH)
        vtok = at("vtok", [P, NT, D], F32, offset=O_ACTH + 2 * HEADS * L)
        O_OT = O_ACTH + 2 * HEADS * L + NT * D
        oH = at("oH", [P, CT, L], F32R, offset=O_OT)
        oL = at("oL", [P, CT, L], F32R, offset=O_OT + CT * L)
        assert O_OT + 2 * CT * L <= O_ACTL + FT * L
        o_att = [O_HG]

        def att(name, shape, dt=F32):
            t = at(name, shape, dt, offset=o_att[0])
            o_att[0] += -(-int(np.prod(shape[1:])) // 8) * 8
            assert o_att[0] <= O_ACTH
            return t

        Pb = att("Pb", [P, 2, L])
        Ab = att("Ab", [P, L])
        AT = att("AT", [P, NT, P])
        Ob = att("Ob", [P, NT, P])
        On = att("On", [P, NT, P])
        qs = att("qs", [P, L])
        ks = att("ks", [P, L])
        identB = att("identB", [P, P], mybir.dt.bfloat16)
        maskB = att("maskB", [P, P], mybir.dt.bfloat16)
        osq = att("osq", [P, P])
        ytok = at("ytok", [P, SEQ // P, D], F32, offset=O_HG)
        ysq = at("ysq", [P, P], F32, offset=O_HG + 4 * D)
        END = (229344 - WORDS0) // 4
        assert top[0] <= END, (top[0], END)

        ident, swap64, swap32, mask = (cst[:, i * P:(i + 1) * P] for i in range(4))
        sgn, nsgn = cst[:, 512:513], cst[:, 513:514]

        ps = ctx.enter_context(nc.psum_tensor("ps", [P, 8, 512], F32))

        def pspan(slot, spans):
            return ps[:, 2 * slot:2 * slot + 2, 0:spans[0][1]]

        def span(ap, spans):
            t0, w = spans[0]
            return ap[:, t0:t0 + 2 * w].rearrange("p (a b) -> p a b", a=2)

        def score_row(c, nq, nk):
            return ps[0:nq, 2 * c:2 * c + 2].rearrange("p a b -> p (a b)")[:, PS_COL:PS_COL + nk]

        turned_row = ps[:, 6:8].rearrange("p a b -> p (a b)")[:, 512 - META:512 - META + L]

        raw_in = [sem(f"raw_in{i}") for i in range(2)]
        w_hi = sem("w_hi")
        w_lo = sem("w_lo")
        w_used = sem("w_used")

        glu_w = inp["s5_w_glu"]
        qkv_w, wo_w = inp["attn_w_qkv"], inp["attn_w_o"]
        up_w, down_w = inp["ffn_w_up"], inp["ffn_w_down"]

        def cols(mat, c0, r0=0, nk=8):
            return mat[r0:r0 + nk * P, ds(c0, P)].rearrange("(k p) c -> p k c", p=P)

        def load_unit(sp, n, src, slot, nk=8):
            if not isinstance(n, int) or n >= 2:
                sp.wait_ge(w_lo, n - 1)
            sp.dma_start(raw[:, slot % 2, 0:nk, :], src).then_inc(raw_in[slot % 2], 16)

        def split_hi(act, n, slot, half, nk=8):
            act.wait_ge(raw_in[slot % 2], half * 16 + 16)
            if not isinstance(n, int) or n >= 4:
                act.wait_ge(w_used, n - 3)
            nc.scalar.activation(wH[:, slot, 0:nk], raw[:, slot % 2, 0:nk], ACT.Copy).then_inc(w_hi, 1)

        def split_lo(pool, n, slot, nk=8):
            pool.wait_ge(w_hi, n + 1)
            nc.gpsimd.tensor_tensor(wL[:, slot, 0:nk], raw[:, slot % 2, 0:nk], wH[:, slot, 0:nk].bitcast(F32),
                                    ALU.subtract).then_inc(w_lo, 1)

        def unit_products(pe, n, slot, bank, xH, xL, spans, kt0, nk, first, last, ready=None):
            pe.wait_ge(w_hi, n + 1)
            pe.wait_ge(w_lo, n + 1)
            for k in range(nk):
                kt = kt0 + k
                if ready is not None:
                    ready(kt)
                for w, x, s0, s1 in ((wH, xH, True, False), (wH, xL, False, False), (wL, xH, False, True)):
                    for b, (t0, tw) in enumerate(spans):
                        mm = nc.tensor.matmul(ps[:, bank + b, 0:tw], w[:, slot, k, :], x[:, kt, t0:t0 + tw],
                                              start=first and k == 0 and s0,
                                              stop=last and k == nk - 1 and s1)
            mm.then_inc(w_used, 1)

        O = [O_HG]

        def s5(name, shape, dt=F32):
            words = -(-int(np.prod(shape[1:])) // 8) * 8
            for r in regions:
                if r[1] - r[0] >= words:
                    o = r[0]
                    r[0] += words
                    return nc.alloc_sbuf_tensor_at(name, list(shape), dt, offset=WORDS0 + 4 * o)
            raise AssertionError((name, words, regions))

        regions = [[O_HG, O_ACTH], [O_ACTH + CT * L, O_ACTL], [O_ACTL + CT * L, O_ACTL + FT * L],
                   [O_WH + 2048, O_WH + 4096], [O_WL + 2048, O_WL + 4096], [O_SPARE, END],
                   [O_SCR + 128, O_SCR + 128 + 3 * L + 2 * (L + 2) + 2 * L - 8]]
        o_x2 = regions[0][0]
        X2 = at("X2", [NK, T, D], F32, offset=o_x2)
        TT = s5("TT", [P, 2, BG, P])
        Kp = s5("Kp", [GC, BG, 15 * GC])
        Z2 = s5("Z2", [NK, T, P])
        rt1 = s5("rt1", [P, BG, NK])
        rt2 = s5("rt2", [P, BG, NK])
        zin = s5("zin", [P, BG, NK])
        zst = s5("zst", [P, BG, NK])
        Sst = s5("Sst", [P, BG, NK])
        assert regions[0][0] - o_x2 <= 8192
        regions[0][0] = max(regions[0][0], o_x2 + 8192)
        o_bn = regions[1][0]
        Bn = at("Bn", [G, 2, D], F32, offset=o_bn)
        Cn = at("Cn", [P, CT, 2, NST], F32, offset=o_bn + 2048)
        E = s5("E", [P, 2, BG, T + 1, GC])
        F = s5("F", [P, BG, T, GC])
        assert regions[1][0] - o_bn >= 3072
        Bst = s5("Bst", [P, G, GC])
        Bsw = s5("Bsw", [P, G, GC])
        Q1 = s5("Q1", [P, G, GC])
        Q2 = s5("Q2", [P, G, GC])
        WBT = s5("WBT", [P, BG, P])
        xb = s5("xb", [NK, 2, T, P])
        xn = s5("xn", [NK, BG, T, GC])
        U = s5("U", [P, 2, BG, NK])
        P1 = s5("P1", [P, T + 1, G])
        P2 = s5("P2", [P, T + 1, G])
        PR1 = s5("PR1", [P, T, G])
        PR2 = s5("PR2", [P, T, G])
        TA1 = s5("TA1", [P, G, 8])
        TA2 = s5("TA2", [P, G, 8])
        TB1 = s5("TB1", [P, G, 9])
        TB2 = s5("TB2", [P, G, 9])
        T1 = s5("T1", [P, 2, BG, 72])
        T2 = s5("T2", [P, 2, BG, 72])
        R = s5("R", [P, BG, NK])
        tmpE = s5("tmpE", [P, 1152])
        tmpP = s5("tmpP", [P, 1024])
        gainJ = s5("gainJ", [P, G])
        dT = s5("dT", [GC, G])
        an = s5("an", [G, 2, 2, NST])
        gd = s5("gd", [G, T + 1, GC])
        rho = s5("rho", [P, G])
        ssq = s5("ssq", [NK, 3, T])
        scr = at("scr", [P, 4, D], F32, offset=O_ACTL)
        junk = at("junk", [P, D], F32, offset=O_ACTH)
        pw = at("pw", [P, 18, G], F32, offset=O_ACTH + D)
        sm = at("sm", [P, 32, G], F32, offset=O_ACTH + D + 18 * G)
        eps_col = tiny[:, 0:1]
        nlam = tiny[:, 1:2]
        lam_s = tiny[:, 2:4]
        lam_e = tiny[:, 4:6]
        mx, nm, esum = tiny[:, 8:10], tiny[:, 10:12], tiny[:, 12:14]
        ratio = tiny[:, 14:15]
        inv = tiny[:, 16:26].rearrange("p (i c) -> p i c", c=2)
        hsq, hrt, hinv = tiny[:, 32:37], tiny[:, 40:45], tiny[:, 48:53]
        sub_gain = tiny[:, 56:57]
        ysum = tiny[:, 64:96]
        ytot, yrt, yinv = tiny[:, 96:100], tiny[:, 100:104], tiny[:, 104:108]
        lam = tiny[:, 128:384]

        s_const = sem("s_const")
        s_x2 = sem("s_x2")
        s_an = sem("s_an")
        s_bn = sem("s_bn")
        s_cn = sem("s_cn")
        s_vec = sem("s_vec")
        s_dt = sem("s_dt")
        ones_set = sem("ones_set")
        pro_ps = sem("pro_ps")
        pro_act = sem("pro_act")
        dve_seq = sem("dve_seq")
        pool_seq = sem("pool_seq")
        act_seq = sem("act_seq")
        xb_in = [sem(f"xb_in{i}") for i in range(2)]
        xn_set = sem("xn_set")
        xt_ps = sem("xt_ps")
        xt_out = sem("xt_out")
        u_ps = sem("u_ps")
        u_set = sem("u_set")
        f_set = sem("f_set")
        ft_ps = sem("ft_ps")
        wbt_set = sem("wbt_set")
        e_set = sem("e_set")
        k_ps = sem("k_ps")
        k_copied = sem("k_copied")
        kp_set = sem("kp_set")
        tt_in = [sem(f"tt_in{i}") for i in range(2)]
        v_ps = sem("v_ps")
        v_read = sem("v_read")
        z_scanned = sem("z_scanned")
        zsw_ps = sem("zsw_ps")
        s_set = sem("s_set")
        y_ps = sem("y_ps")
        gelu_set = sem("gelu_set")
        zt_ps = sem("zt_ps")
        z_hi = sem("z_hi")
        z_lo = sem("z_lo")
        t1_set = sem("t1_set")

        glu_sig = sem("glu_sig")
        glu_free = sem("glu_free")
        h_new = [sem(f"h_new{i}") for i in range(4)]
        hg_hi = [sem(f"hg_hi{i}") for i in range(3)]
        hg_lo = [sem(f"hg_lo{i}") for i in range(3)]
        sq_sum = [sem(f"sq_sum{i}") for i in range(3)]
        stat_ps = [sem(f"stat_ps{i}") for i in range(3)]
        stat_sqrt = [sem(f"stat_sqrt{i}") for i in range(3)]
        up_free = [sem(f"up_free{i}") for i in range(2)]
        conv_gate = [sem(f"conv_gate{i}") for i in range(2)]
        silu_set = [sem(f"silu_set{i}") for i in range(2)]
        act_set = [sem(f"act_set{i}") for i in range(2)]
        act_hi = [sem(f"act_hi{i}") for i in range(2)]
        act_lo = [sem(f"act_lo{i}") for i in range(2)]
        pro_act_dt = sem("pro_act_dt")
        pro_dve_a = sem("pro_dve_a")
        pv_set = sem("pv_set")
        x_ssq = sem("x_ssq")
        x_sqrt = sem("x_sqrt")
        xr_set = sem("xr_set")
        kp_zero = sem("kp_zero")
        w_phasor = sem("w_phasor")
        b_scaled = sem("b_scaled")
        t_base = sem("t_base")
        powers = sem("powers")
        cs_in = sem("cs_in")
        lam_in = sem("lam_in")
        fgain_in = sem("fgain_in")
        lam_sum = sem("lam_sum")
        lam_exp = sem("lam_exp")
        rope_sw = sem("rope_sw")
        rope_cos = sem("rope_cos")
        qk_set = sem("qk_set")
        v_zero = sem("v_zero")
        v_norm = sem("v_norm")
        v_turned = sem("v_turned")
        v_set = sem("v_set")
        mask_set = sem("mask_set")
        head_in = sem("head_in")
        sc_ps = sem("sc_ps")
        max_set = sem("max_set")
        probs_set = sem("probs_set")
        diff_set = sem("diff_set")
        pt_ps = sem("pt_ps")
        at_set = sem("at_set")
        o_ps = sem("o_ps")
        o_set = sem("o_set")
        o_sq = sem("o_sq")
        sub_root = sem("sub_root")
        on_set = sem("on_set")
        ot_ps = sem("ot_ps")
        o_hi = sem("o_hi")
        o_lo = sem("o_lo")
        yt_ps = sem("yt_ps")
        y_set = sem("y_set")
        y_sqs = sem("y_sqs")
        y_root = sem("y_root")
        y_out = sem("y_out")
        out_done = sem("out_done")

        block = ctx.enter_context(nc.Block())

        def ffn_loads(sp, l):
            nu, nd = (U_UP0, U_DN0) if l == 0 else (U_UP1, U_DN1)
            with sp.Fori(0, FT // 2) as i:
                for c in range(4):
                    load_unit(sp, i * 4 + (nu + c), cols(up_w[l], i * (2 * P) + ((c % 2) * FF + (c // 2) * P)), c)
            with sp.Fori(0, 2) as i:
                for c in range(12):
                    kc, nk = c % 3, (8, 8, 6)[c % 3]
                    load_unit(sp, i * 12 + (nd + c),
                              cols(down_w[l], i * (4 * P) + (c // 3) * P, kc * D, nk), c, nk)

        @block.sync
        def _(sp):
            sp.dma_start(cst[:, :], consts[:, 0:514]).then_inc(s_const, 16)
            sp.dma_start(X2[0:2], inp["meta_tokens"].rearrange("(k j) d -> k j d", j=T)).then_inc(s_x2, 16)
            sp.dma_start(X2[2:NK], inp["x"][0].rearrange("(k j) d -> k j d", j=T)).then_inc(s_x2, 16)
            for i in range(2):
                load_unit(sp, i, cols(glu_w[0], (i % 2) * D), i)

            def load_xb(b, par):
                sp.dma_start(xb[0:2, par], inp["meta_tokens"][:, ds(b * P, P)]
                             .rearrange("(k j) d -> k j d", j=T)).then_inc(xb_in[par], 16)
                sp.dma_start(xb[2:NK, par], inp["x"][0][:, ds(b * P, P)]
                             .rearrange("(k j) d -> k j d", j=T)).then_inc(xb_in[par], 16)

            def toeplitz(b, par):
                sp.wait_ge(kp_set, b + 1)
                if not isinstance(b, int) or b >= 2:
                    sp.wait_ge(y_ps, b - 1)
                for i in range(T):
                    sp.dma_start(TT[i * GC:(i + 1) * GC, par],
                                 Kp[:, :, (T - 1 - i) * GC:(T - 1 - i) * GC + P]).then_inc(tt_in[par], 16)

            load_xb(0, 0)
            load_xb(1, 1)
            toeplitz(0, 0)
            toeplitz(1, 1)
            with sp.Fori(0, 3) as i:
                for par in range(2):
                    b = i * 2 + (par + 2)
                    sp.wait_ge(u_ps, b - 1)
                    sp.wait_ge(xn_set, b - 1)
                    load_xb(b, par)
                    toeplitz(b, par)
            for n in range(2, 16):
                load_unit(sp, n, cols(glu_w[0], (n % 2) * D + (n // 2) * P), n)
            ffn_loads(sp, 0)
            sp.dma_start(cs[:, :].rearrange("p a t -> p (a t)"), consts[:, 514:514 + 2 * L]).then_inc(cs_in, 16)
            with sp.Fori(0, 6) as i:
                for c in range(4):
                    load_unit(sp, i * 4 + (U_QKV + c), cols(qkv_w[0], i * (4 * P) + c * P), c)
            with sp.Fori(0, 2) as i:
                for c in range(4):
                    load_unit(sp, i * 4 + (U_WO + c), cols(wo_w[0], i * (4 * P) + c * P), c)
            ffn_loads(sp, 1)
            for t in range(SEQ // P):
                sp.wait_ge(y_out, t + 1)
                sp.dma_start(out[0][t * P:(t + 1) * P, :], ytok[:, t]).then_inc(out_done, 16)
            sp.wait_ge(out_done, 16 * (SEQ // P))

        @block.tensor
        def _(pe):
            pe.wait_ge(s_const, 16)
            pe.wait_ge(s_an, 96)
            for i, (src, n) in enumerate(((an[:, 0].rearrange("g a n -> g (a n)"), P),
                                          (an[:, 1].rearrange("g a n -> g (a n)"), P),
                                          (gd[:, 0:T].rearrange("g j c -> g (j c)"), P),
                                          (gd[:, T], GC))):
                mm = nc.tensor.transpose(ps[0:n, 1, i * G:(i + 1) * G], src, ident[0:G, 0:G])
            mm.then_inc(pro_ps, 1)
            pe.wait_ge(s_bn, 32)
            for c in range(GC):
                mm = nc.tensor.transpose(ps[:, 2 + c // 8, (c % 8) * G:(c % 8 + 1) * G],
                                         Bn[:, :, :].rearrange("g a n -> g (a n)")[:, c:2 * D:GC], ident[0:G, 0:G])
            mm.then_inc(pro_ps, 1)
            pe.wait_ge(s_cn, 32)
            for t in range(CT):
                mm = nc.tensor.transpose(ps[:, 4 + t // 4, (t % 4) * P:(t % 4 + 1) * P],
                                         Cn[:, t].rearrange("p a n -> p (a n)"), ident)
            mm.then_inc(pro_ps, 1)
            pe.wait_ge(s_vec, 16 * 8)
            for t, rows in enumerate((P, P, 96, 49)):
                mm = nc.tensor.transpose(ps[:, 0, t * P:t * P + rows], vstage[0:rows, t], ident[0:rows, 0:rows])
            mm.then_inc(pro_ps, 1)
            pe.wait_ge(pro_act, 1)
            for h in range(2):
                mm = nc.tensor.matmul(ps[:, 6 + h, :], swap64, Bst[:, 32 * h:32 * h + 32], start=True, stop=True)
            mm.then_inc(pro_ps, 1)
            pe.wait_ge(pro_act, 2)
            for h in range(2):
                mm = nc.tensor.matmul(ps[:, 2 + h, :], swap64, Q1[:, 32 * h:32 * h + 32], start=True, stop=True)
            mm.then_inc(pro_ps, 1)

            def x_transposes(b, par):
                pe.wait_ge(xb_in[par], b16(b, par))
                if not isinstance(b, int) or b >= 2:
                    pe.wait_ge(z_lo, b - 1)
                elif b == 0:
                    pe.wait_ge(pro_act, 3)
                for j in range(T):
                    mm = nc.tensor.transpose(ps[:, j // 4, (j % 4) * NK:(j % 4 + 1) * NK],
                                             xb[:, par, j], ident[0:NK, 0:NK])
                mm.then_inc(xt_ps, 1)

            def b16(b, par):
                return (b - par) * 16 + 32

            def u_transposes(b, par):
                pe.wait_ge(xn_set, b + 1)
                if not isinstance(b, int) or b >= 1:
                    pe.wait_ge(v_read, b)
                else:
                    pe.wait_ge(pro_act, 3)
                for g in range(BG):
                    mm = nc.tensor.transpose(ps[:, 4 + g // 4, (g % 4) * NK:(g % 4 + 1) * NK],
                                             xn[:, g].rearrange("k j c -> k (j c)"), ident[0:NK, 0:NK])
                mm.then_inc(u_ps, 1)
                pe.wait_ge(f_set, b + 1)
                for g in range(BG):
                    mm = nc.tensor.transpose(ps[:, 2 + g // 4, (g % 4) * P:(g % 4 + 1) * P],
                                             F[:, g].rearrange("p j c -> p (j c)"), ident)
                mm.then_inc(ft_ps, 1)

            def kernel_products(b, par):
                pe.wait_ge(e_set, b + 1)
                pe.wait_ge(u_set, b + 1)
                for g in range(BG):
                    mm = nc.tensor.matmul(ps[0:GC, 4 + g // 4, (g % 4) * P:(g % 4 + 1) * P],
                                          F[:, g, T - 1], E[:, par, g, 0:T], start=True, stop=True)
                mm.then_inc(k_ps, 1)

            def inject(b, par):
                pe.wait_ge(wbt_set, b + 1)
                pe.wait_ge(k_copied, b + 1)
                for g in range(BG):
                    for sw in range(2):
                        for half in range(2):
                            mm = nc.tensor.matmul(
                                ps[64 * half:64 * half + 64, 2 + 2 * sw + g // 4, (g % 4) * NK:(g % 4 + 1) * NK],
                                WBT[:, g, 64 * (half ^ sw):64 * (half ^ sw) + 64], U[:, par, g],
                                start=True, stop=True)
                mm.then_inc(v_ps, 1)

            def swapped_states(b):
                pe.wait_ge(z_scanned, b + 1)
                if not isinstance(b, int) or b >= 1:
                    pe.wait_ge(gelu_set, b)
                for h in range(2):
                    mm = nc.tensor.matmul(ps[:, 6 + h, 0:4 * NK], swap64, zst[:, 4 * h:4 * h + 4],
                                          start=True, stop=True)
                mm.then_inc(zsw_ps, 1)

            def outputs(b, par, done):
                pe.wait_ge(s_set, b + 1)
                pe.wait_ge(tt_in[par], done)
                for g in range(BG):
                    o = ps[0:NK, 6 + g // 4, (g % 4) * P:(g % 4 + 1) * P]
                    nc.tensor.matmul(o, Sst[:, g], E[:, par, g, 1:T + 1], start=True, stop=False)
                    mm = nc.tensor.matmul(o, U[:, par, g], TT[:, par, g], start=False, stop=True)
                mm.then_inc(y_ps, 1)

            def z_transposes(b):
                pe.wait_ge(gelu_set, b + 1)
                for j in range(T):
                    mm = nc.tensor.transpose(ps[:, j // 4, (j % 4) * NK:(j % 4 + 1) * NK],
                                             Z2[:, j], ident[0:NK, 0:NK])
                mm.then_inc(zt_ps, 1)

            x_transposes(0, 0)
            u_transposes(0, 0)
            kernel_products(0, 0)

            def step(b, par, more):
                inject(b, par)
                if more:
                    x_transposes(b + 1, 1 - par)
                    u_transposes(b + 1, 1 - par)
                swapped_states(b)
                if more:
                    kernel_products(b + 1, 1 - par)
                outputs(b, par, (b - par) * 64 + 128)
                if more:
                    pe.wait_ge(xt_out, b + 2)
                z_transposes(b)

            step(0, 0, True)
            step(1, 1, True)
            with pe.Fori(0, 2) as i:
                for par in range(2):
                    step(i * 2 + (par + 2), par, True)
            step(6, 0, True)
            step(7, 1, False)

            def stat_products(i):
                pe.wait_ge(sq_sum[i], CT)
                for b in range(2):
                    mm = nc.tensor.matmul(ps[:, 6 + b, 0:264], ones[:, :], acc[:, 264 * b:264 * b + 264],
                                          start=True, stop=True)
                mm.then_inc(stat_ps[i], 1)

            def hg_ready(i):
                def ready(kt):
                    pe.wait_ge(hg_hi[i], kt + 1)
                    pe.wait_ge(hg_lo[i], kt + 1)
                return ready

            def z_ready(kt):
                pe.wait_ge(z_lo, kt + 1)

            def glu():
                with pe.Fori(0, 4) as i:
                    for q in range(2):
                        pe.wait_ge(glu_free, i * 2 + q)
                        for c in range(2):
                            unit_products(pe, i * 4 + 2 * q + c, 2 * q + c, (4, 0)[q] + 2 * c, actH, actL, ALL,
                                          0, 8, True, True, z_ready if c == 0 and q == 0 else None)

            def ffn(l, spans, spans_down):
                nu, nd = (U_UP0, U_DN0) if l == 0 else (U_UP1, U_DN1)
                stat_products(2 * l)
                with pe.Fori(0, FT // 2) as i:
                    for q in range(2):
                        pe.wait_ge(up_free[l], i * 2 + q)
                        for c in range(2):
                            unit_products(pe, i * 4 + (nu + 2 * q + c), 2 * q + c, 4 * q + 2 * c, hgH, hgL, spans,
                                          0, 8, True, True, hg_ready(2 * l) if q == 0 and c == 0 else None)
                pe.wait_ge(up_free[l], FT)
                with pe.Fori(0, 2) as i:
                    for m in range(4):
                        pe.wait_ge(h_new[1 + 2 * l], i * 4 + (m - 1) if m else i * 3)
                        for kc in range(3):
                            def ready(kt):
                                pe.wait_ge(act_hi[l], kt + 1)
                                pe.wait_ge(act_lo[l], kt + 1)
                            nk = (8, 8, 6)[kc]
                            unit_products(pe, i * 12 + (nd + 3 * m + kc), (3 * m + kc) % 4, 2 * (m % 2), actH, actL,
                                          spans_down, 8 * kc, nk, kc == 0, kc == 2, ready if m == 0 else None)
                        if l == 1 and m:
                            y_transposes(i * 4, i * 4 + m, m - 1)
                    if l == 1:
                        y_transposes(i * 4, i * 4 + 4, 3)

            def y_transposes(ct, n, m):
                pe.wait_ge(h_new[3], n)
                free = n - 2 if m else ct
                pe.wait_ge(y_set, free)
                pe.wait_ge(y_sqs, free * 4)
                for t in range(SEQ // P):
                    mm = nc.tensor.transpose(ps[:, 4 + m % 2, t * P:(t + 1) * P],
                                             (cg, cv)[m % 2][:, t * P:(t + 1) * P], ident)
                mm.then_inc(yt_ps, 1)

            def qkv():
                stat_products(1)
                with pe.Fori(0, 4) as i:
                    for m in range(4):
                        pe.wait_ge(qk_set, i * 4 + m)
                        unit_products(pe, i * 4 + (U_QKV + m), m, 2 * (m % 2), hgH, hgL, ALL, 0, 8, True, True,
                                      hg_ready(1) if m == 0 else None)

                def v_transposes(n, m):
                    pe.wait_ge(v_norm, n)
                    pe.wait_ge(v_set, n - 2 if m else n - 1)
                    for t, (t0, tn) in enumerate(TILES):
                        o = (ps[0:tn, 5 + 2 * (m % 2), 0:P] if t == 0 else
                             ps[:, 4 + 2 * (m % 2), (t - 1) * P:t * P])
                        mm = nc.tensor.transpose(o, (cg, cv)[m % 2][:, t0:t0 + tn], ident)
                    mm.then_inc(v_turned, 1)

                pe.wait_ge(qk_set, 2 * HEADS + 1)
                with pe.Fori(0, 2) as i:
                    for m in range(4):
                        n = i * 4 + m
                        pe.wait_ge(v_norm, n - 1 if m else i * 3)
                        unit_products(pe, n + (U_QKV + 2 * HEADS), m, 2 * (m % 2), hgH, hgL, ALL, 0, 8, True, True)
                        if m:
                            v_transposes(n, m - 1)
                    v_transposes(i * 4 + 4, 3)

            def scores(h, i, n):
                q0, nq = TILES[i]
                nk = q0 + nq
                for c in range(2):
                    if not isinstance(n, int) or n:
                        pe.wait_ge(probs_set, n * 2 + (c - 1))
                    if c == 0 and i == 0:
                        pe.wait_ge(head_in, h + 1)
                    half = slice(HD * c, HD * c + HD)
                    pieces = [(0, PS_COL, 0, min(nk, CUT))] + ([(1, -CUT, CUT, nk)] if nk > CUT else [])
                    for bank, col, a, b in pieces:
                        nc.tensor.matmul(ps[:, 2 * c + bank, a + col:b + col], qs[half, q0:q0 + P], ks[half, a:b],
                                         start=True, stop=b < nk)
                    nc.tensor.matmul(ps[:, 2 * c + bank, q0 + col:nk + col], identB[0:nq], maskB[0:nq, 0:nq],
                                     start=False, stop=True).then_inc(sc_ps, 1)

            def attend(h, n, i, first=False, last=False):
                q0, nq = TILES[i]
                if not (last and i == NT - 1):
                    scores(h + 1 if i == NT - 1 else h, (i + 1) % NT, n + 1)
                pe.wait_ge(diff_set, n + 1)
                pe.wait_ge(o_set, n)
                for t in (*range(1, i + 1), 0):
                    k0, kn = TILES[t]
                    o = ps[0:kn, 5, 0:P] if t == 0 else ps[:, 4, (t - 1) * P:t * P]
                    mm = nc.tensor.transpose(o, Ab[:, k0:k0 + kn], ident)
                mm.then_inc(pt_ps, 1)
                if i == 1 and not first:
                    turn_head(h - 1)
                pe.wait_ge(at_set, n + 1)
                for t in (*range(1, i + 1), 0):
                    kn = P if i == 0 else TILES[t][1]
                    mm = nc.tensor.matmul(ps[:, 5, P:2 * P], AT[0:kn, t, :], vtok[0:kn, t, ds(h * P, P)],
                                          start=t == min(i, 1), stop=t == 0)
                mm.then_inc(o_ps, 1)

            def turn_head(h):
                pe.wait_ge(on_set, h + 1)
                pe.wait_ge(o_lo, h)
                for t in (*range(1, NT), 0):
                    tn = TILES[t][1]
                    o = ps[:, 6, 512 - META:512] if t == 0 else ps[:, 7, (t - 1) * P:t * P]
                    mm = nc.tensor.transpose(o, On[0:tn, t], ident[0:tn, 0:tn])
                mm.then_inc(ot_ps, 1)

            def attention():
                pe.wait_ge(mask_set, 1)
                pe.wait_ge(v_norm, HEADS)
                scores(0, 0, 0)
                pe.wait_ge(v_set, HEADS)
                for i in range(NT):
                    attend(0, i, i, first=True)
                with pe.Fori(0, HEADS - 2) as h:
                    for i in range(NT):
                        attend(h + 1, h * NT + (NT + i), i)
                for i in range(NT):
                    attend(HEADS - 1, (HEADS - 1) * NT + i, i, last=True)
                turn_head(HEADS - 1)

            def out_projection():
                def ready(kt):
                    pe.wait_ge(o_hi, kt + 1)
                    pe.wait_ge(o_lo, kt + 1)
                with pe.Fori(0, 2) as i:
                    for m in range(4):
                        pe.wait_ge(h_new[2], i * 4 + (m - 1) if m else i * 3)
                        unit_products(pe, i * 4 + (U_WO + m), m, 2 * (m % 2), oH, oL, ALL, 0, 8, True, True,
                                      ready if m == 0 else None)

            glu()
            ffn(0, ALL, ALL)
            qkv()
            attention()
            out_projection()
            ffn(1, FROM12, FROM16)

        @block.scalar
        def _(act):
            for c in range(2):
                act.dma_start(an[:, 0, c], inp["s5_a_re"][0]).then_inc(s_an, 16)
                act.dma_start(an[:, 1, c], inp["s5_a_im"][0]).then_inc(s_an, 16)
            act.dma_start(gd[:, 0:T], inp["norm_mix_gain"][0].rearrange("(g c) -> g c", c=GC).unsqueeze(1)
                          .broadcast_to([G, T, GC])).then_inc(s_an, 16)
            act.dma_start(gd[:, T], inp["s5_d"][0].rearrange("(g c) -> g c", c=GC)).then_inc(s_an, 16)
            act.dma_start(sm[:, 0], inp["s5_log_dt"].broadcast_to([P, G])).then_inc(s_dt, 16)
            act.dma_start(Bn[:, 0], inp["s5_b_re"][0].rearrange("g n c -> g (n c)")).then_inc(s_bn, 16)
            act.dma_start(Bn[:, 1], inp["s5_b_im"][0].rearrange("g n c -> g (n c)")).then_inc(s_bn, 16)
            for c, name in enumerate(("s5_c_re", "s5_c_im")):
                act.dma_start(Cn[:, :, c], inp[name][0].rearrange("(t g) c n -> (g c) t n", t=CT)).then_inc(s_cn, 16)
            act.dma_start(lam, inp["attn_lambda"][0].rearrange("a b -> (a b)").unsqueeze(0)
                          .broadcast_to([P, 4 * HD])).then_inc(lam_in, 16)
            cw = inp["ffn_conv_w"].rearrange("l j (t p) -> (l j t) p", p=P)
            rows = lambda a: a.rearrange("l (t p) -> (l t) p", p=P)
            for t, r0, src in ((0, 0, cw[0:P]), (1, 0, cw[P:2 * P]), (2, 0, cw[2 * P:264]),
                               (2, 8, rows(inp["ffn_conv_b"])), (3, 0, rows(inp["norm_mix_gain"])),
                               (3, 16, rows(inp["norm_ffn_gain"])), (3, 32, rows(inp["s5_b_glu"])),
                               (3, 48, inp["attn_subln_gain"])):
                act.dma_start(vstage[r0:r0 + src.shape[0], t], src).then_inc(s_vec, 16)

            act.wait_ge(s_dt, 16)
            nc.scalar.activation(sm[:, 1], sm[:, 0], ACT.Exp).then_inc(pro_act_dt, 1)
            act.wait_ge(pro_ps, 2)
            for h in range(2):
                bps = ps[:, 2 + h, :].rearrange("p (c g) -> p g c", c=8)
                ins = nc.scalar.activation(Bst[:, :, 8 * h:8 * h + 8], bps, ACT.Copy)
            ins.then_inc(pro_act, 1)
            act.wait_ge(pro_ps, 3)
            for h in range(2):
                ins = nc.scalar.activation(Q1[:, 32 * h:32 * h + 32], ps[:, 4 + h, :], ACT.Copy, scale=sgn)
            ins.then_inc(pro_act, 1)
            act.wait_ge(pro_dve_a, 1)
            nc.scalar.activation(sm[:, 2], sm[:, 9], ACT.Exp)
            nc.scalar.activation(rho[:, :], sm[:, 9], ACT.Exp, scale=8.0)
            act.wait_ge(pro_dve_a, 2)
            nc.scalar.activation(sm[:, 4], sm[:, 10], ACT.Sin)
            nc.scalar.activation(sm[:, 5], sm[:, 6], ACT.Sin).then_inc(pro_act_dt, 1)
            act.wait_ge(pro_ps, 4)
            nc.scalar.activation(PV[:, 0:352], ps[:, 0, 0:352], ACT.Copy)
            nc.scalar.activation(PV[:, 352:401], ps[:, 0, 384:433], ACT.Copy).then_inc(pv_set, 1)
            act.wait_ge(pro_ps, 5)
            for h in range(2):
                ins = nc.scalar.activation(Bsw[:, 32 * h:32 * h + 32], ps[:, 6 + h, :], ACT.Copy)
            act.wait_ge(pro_ps, 6)
            for h in range(2):
                ins = nc.scalar.activation(Q2[:, 32 * h:32 * h + 32], ps[:, 2 + h, :], ACT.Copy, scale=-1.0)
            ins.then_inc(pro_act, 1)
            act.wait_ge(s_x2, 32)
            for j in range(T // 2):
                nc.scalar.activation(junk[0:NK], X2[:, j], ACT.Square,
                                     accum_out=ssq[:, 0, j:j + 1]).then_inc(act_seq, 1)
                act.wait_ge(act_seq, j + 1)
            act.wait_ge(x_ssq, 1)
            nc.scalar.activation(ssq[:, 2], ssq[:, 1], ACT.Sqrt).then_inc(x_sqrt, 1)
            for n in range(2):
                split_hi(act, n, n, 0)

            def turn_out(b, par):
                act.wait_ge(xt_ps, b + 1)
                for h in range(2):
                    o = hT[:, ds(b, 1)].rearrange("p a (k j) -> p (a j) k", j=T)[:, 4 * h:4 * h + 4]
                    ins = nc.scalar.activation(o, ps[:, h, 0:4 * NK].rearrange("p (j k) -> p j k", j=4), ACT.Copy)
                ins.then_inc(xt_out, 1)
                act.wait_ge(ft_ps, b + 1)
                if not isinstance(b, int) or b >= 1:
                    act.wait_ge(v_ps, b)
                for h in range(2):
                    ins = nc.scalar.activation(WBT[:, 4 * h:4 * h + 4], ps[:, 2 + h, :], ACT.Copy)
                ins.then_inc(wbt_set, 1)

            def kernel_out(b, par):
                act.wait_ge(k_ps, b + 1)
                if not isinstance(b, int) or b >= 1:
                    act.wait_ge(tt_in[1 - par], tt_done(b - 1, 1 - par))
                else:
                    act.wait_ge(kp_zero, 1)
                for h in range(2):
                    ins = nc.scalar.activation(
                        Kp[:, 4 * h:4 * h + 4, 7 * GC:15 * GC],
                        ps[0:GC, 4 + h, :].rearrange("p (g c) -> p g c", g=4), ACT.Copy)
                ins.then_inc(k_copied, 1)

            def tt_done(b, par):
                return (b - par) * 64 + 128

            def gelu(b):
                act.wait_ge(y_ps, b + 1)
                if not isinstance(b, int) or b >= 1:
                    act.wait_ge(zt_ps, b)
                for h in range(2):
                    o = Z2[:, :, 64 * h:64 * h + 64].rearrange("k j (g c) -> k g j c", g=4)
                    ins = nc.scalar.activation(
                        o, ps[0:NK, 6 + h, :].rearrange("k (g j c) -> k g j c", g=4, j=T), ACT.Gelu_apprx_tanh)
                ins.then_inc(gelu_set, 1)

            def z_round(b):
                act.wait_ge(zt_ps, b + 1)
                for h in range(2):
                    o = actH[:, ds(b, 1)].rearrange("p a (k j) -> p (a j) k", j=T)[:, 4 * h:4 * h + 4]
                    ins = nc.scalar.activation(o, ps[:, h, 0:4 * NK].rearrange("p (j k) -> p j k", j=4), ACT.Copy)
                ins.then_inc(z_hi, 1)

            turn_out(0, 0)
            kernel_out(0, 0)

            def step(b, par, more):
                if more:
                    turn_out(b + 1, 1 - par)
                    kernel_out(b + 1, 1 - par)
                gelu(b)
                z_round(b)

            step(0, 0, True)
            step(1, 1, True)
            with act.Fori(0, 2) as i:
                for par in range(2):
                    step(i * 2 + (par + 2), par, True)
            step(6, 0, True)
            step(7, 1, False)

            def round_hg(i, ct, gain, count):
                act.wait_ge(h_new[count[0]], count[1])
                nc.scalar.activation(hgH[:, ds(ct, 1)], hT[:, ds(ct, 1)], ACT.Copy,
                                     scale=PV[:, ds(gain, 1)]).then_inc(hg_hi[i], 1)

            def glu():
                act.wait_ge(z_lo, CT)
                for n in (2, 3):
                    split_hi(act, n, n, 1)
                with act.Fori(0, 4) as i:
                    for q in range(2):
                        n = i * 4 + 2 * q
                        for c in range(2):
                            split_hi(act, n + (4 + c), 2 * q + c, i * 2 + (2 + q))
                        act.wait_ge(w_used, n + 2)
                        gate = ps[:, (6, 2)[q]:(6, 2)[q] + 2, 0:264]
                        nc.scalar.activation(span(cg, ALL), gate, ACT.Sigmoid,
                                             bias=PV[:, ds(i * 2 + (B_GLU + 8 + q), 1)]).then_inc(glu_sig, 1)
                        round_hg(0, i * 2 + q, i * 2 + (GAIN_FFN + q), (0, i * 2 + (q + 1)))

            def root(i):
                act.wait_ge(stat_ps[i], 1)
                nc.scalar.activation(span(sqt, ALL), ps[:, 6:8, 0:264], ACT.Sqrt, bias=eps_col,
                                     scale=1.0 / D).then_inc(stat_sqrt[i], 1)

            def ffn(l, spans, t0):
                nu, nd = (U_UP0, U_DN0) if l == 0 else (U_UP1, U_DN1)
                root(2 * l)
                with act.Fori(0, FT // 2) as i:
                    for q in range(2):
                        for c in range(2):
                            split_hi(act, i * 4 + (nu + 4 + 2 * q + c), 2 * q + c, i * 2 + (nu // 2 + 2 + q))
                        act.wait_ge(conv_gate[l], i * 2 + (q + 1))
                        nc.scalar.activation(cg[:, t0:], cg[:, t0:], ACT.Silu).then_inc(silu_set[l], 1)
                        act.wait_ge(act_set[l], i * 2 + (q + 1))
                        nc.scalar.activation(actH[:, ds(i * 2 + q, 1), t0:], cg[:, t0:].unsqueeze(1),
                                             ACT.Copy).then_inc(act_hi[l], 1)
                if l == 0:
                    with act.Fori(0, 2) as i:
                        for m in range(4):
                            for c in range(3 * m, 3 * m + 3):
                                split_hi(act, i * 12 + (nd + 4 + c), c % 4, i * 6 + (nd // 2 + 2 + c // 2),
                                         (8, 8, 6)[(c + 4) % 3] if c < 8 else 8)
                            round_hg(1, i * 4 + m, i * 4 + (GAIN_MIX + 8 + m), (1, i * 4 + (m + 1)))
                else:
                    act.wait_ge(w_used, nd)
                    for c in range(20):
                        split_hi(act, nd + 4 + c, c % 4, (nd + 4 + c) // 2, (8, 8, 6)[(c + 4) % 3])
                        if c % 3 == 2:
                            out_squares(c // 3)
                    for n in (6, 7):
                        out_squares(n)
                    act.wait_ge(y_set, CT + 1)
                    nc.scalar.activation(yrt, ytot, ACT.Sqrt, bias=eps_col, scale=1.0 / D).then_inc(y_root, 1)

            def out_squares(n):
                act.wait_ge(y_set, n + 1)
                for t in range(SEQ // P):
                    if n + t:
                        act.wait_ge(y_sqs, 4 * n + t)
                    ins = nc.scalar.activation(ysq[:, :], ps[:, 4 + n % 2, t * P:(t + 1) * P], ACT.Square,
                                               accum_out=ysum[:, 4 * n + t:4 * n + t + 1])
                    ins.then_inc(y_sqs, 1)

            def qkv():
                root(1)
                with act.Fori(0, 4) as i:
                    for m in range(4):
                        split_hi(act, i * 4 + (U_QKV + 4 + m), m, i * 2 + (U_QKV // 2 + 2 + m // 2))
                        act.wait_ge(w_used, i * 4 + (U_QKV + 1 + m))
                        act.wait_ge(qk_set, i * 4 + (m + 1))
                        for q in range(4):
                            r = q ^ 1
                            ins = nc.scalar.activation(span(cg[32 * q:32 * q + 32], ALL),
                                                       ps[32 * r:32 * r + 32, 2 * (m % 2):2 * (m % 2) + 2, 0:264], ACT.Copy)
                        ins.then_inc(rope_sw, 1)
                act.wait_ge(v_zero, 1)
                with act.Fori(0, 2) as i:
                    for m in range(4):
                        split_hi(act, i * 4 + (U_QKV + 20 + m), m, i * 2 + (U_QKV // 2 + 10 + m // 2))
                        act.wait_ge(v_turned, i * 4 + (m + 1))
                        b = 4 + 2 * (m % 2)
                        o = ds((i * 4 + m) * P, P)
                        nc.scalar.activation(vtok[:, 1:NT, o], ps[:, b].rearrange("p (t c) -> p t c", c=P), ACT.Copy)
                        nc.scalar.activation(vtok[0:META, 0:1, o], ps[0:META, b + 1:b + 2, 0:P],
                                             ACT.Copy).then_inc(v_set, 1)

            def exponentials(n, i):
                nq = TILES[i][1]
                nk = sum(TILES[i])
                for c in range(2):
                    act.wait_ge(max_set, n * 2 + (c + 1))
                    if c == 0 and (not isinstance(n, int) or n):
                        act.wait_ge(diff_set, n)
                    nc.scalar.activation(Pb[0:nq, c, 0:nk], score_row(c, nq, nk), ACT.Exp, bias=nm[0:nq, c:c + 1],
                                         scale=SCALE, accum_out=esum[0:nq, c:c + 1]).then_inc(probs_set, 1)

            def attend(h, n, i, first=False, last=False):
                nq = TILES[i][1]
                if not (last and i == NT - 1):
                    exponentials(n + 1, (i + 1) % NT)
                if i == 0 and not first:
                    head_root(h - 1)
                if i == 2 and not first:
                    head_out(h - 1)
                act.wait_ge(o_set, n + 1)
                act.wait_ge(o_sq, n)
                nc.scalar.activation(osq[0:nq], Ob[0:nq, i], ACT.Square,
                                     accum_out=hsq[0:nq, i:i + 1]).then_inc(o_sq, 1)

            def head_root(h):
                act.wait_ge(o_sq, (h + 1) * NT)
                nc.scalar.activation(hrt, hsq, ACT.Sqrt, bias=eps_col, scale=1.0 / P).then_inc(sub_root, 1)

            def head_out(h):
                act.wait_ge(ot_ps, h + 1)
                nc.scalar.activation(oH[:, ds(h, 1)], turned_row.unsqueeze(1), ACT.Copy, scale=sub_gain).then_inc(o_hi, 1)

            def attention():
                act.wait_ge(w_used, U_WO)
                nc.scalar.activation(identB[:, :], ident, ACT.Copy)
                nc.scalar.activation(maskB[:, :], mask, ACT.Copy).then_inc(mask_set, 1)
                act.dma_start(fgain[:, :], inp["final_norm_gain"].unsqueeze(0).broadcast_to([P, D])).then_inc(fgain_in, 16)
                exponentials(0, 0)
                for i in range(NT):
                    attend(0, i, i, first=True)
                with act.Fori(0, HEADS - 2) as h:
                    for i in range(NT):
                        attend(h + 1, h * NT + (NT + i), i)
                for i in range(NT):
                    attend(HEADS - 1, (HEADS - 1) * NT + i, i, last=True)
                head_root(HEADS - 1)
                head_out(HEADS - 1)

            def out_projection():
                with act.Fori(0, 2) as i:
                    for m in range(4):
                        split_hi(act, i * 4 + (U_WO + 4 + m), m, i * 2 + (U_WO // 2 + 2 + m // 2))
                        round_hg(2, i * 4 + m, i * 4 + (GAIN_FFN + 8 + m), (2, i * 4 + (m + 1)))

            glu()
            ffn(0, ALL, 0)
            act.wait_ge(lam_sum, 1)
            nc.scalar.activation(lam_e, lam_s, ACT.Exp).then_inc(lam_exp, 1)
            qkv()
            attention()
            out_projection()
            ffn(1, FROM12, META)

        @block.vector
        def _(dve):
            V = nc.vector
            link = Chain(dve, dve_seq)

            def cmul(e, lk, o, a, b, t):
                e.tensor_tensor(t[0], a[0], b[0], ALU.mult)
                e.tensor_tensor(t[1], a[1], b[1], ALU.mult)
                e.tensor_tensor(t[2], a[1], b[0], ALU.mult)
                lk(e.tensor_tensor(t[3], a[0], b[1], ALU.mult))
                e.tensor_tensor(o[0], t[0], t[1], ALU.subtract)
                lk(e.tensor_tensor(o[1], t[2], t[3], ALU.add))

            V.memset(ones[:, :], 1.0)
            V.memset(eps_col, EPS)
            V.memset(P1[:, 0], 1.0)
            V.memset(P2[:, 0], 0.0).then_inc(ones_set, 1)
            dve.wait_ge(pro_ps, 1)
            V.tensor_copy(sm[:, 7:9], ps[:, 1, 0:2 * G].rearrange("p (a g) -> p a g", a=2))
            V.tensor_copy(gainJ[:, :], ps[:, 1, 2 * G:3 * G])
            link(V.tensor_copy(dT[:, :], ps[0:GC, 1, 3 * G:4 * G]))
            dve.wait_ge(s_const, 16)
            dve.wait_ge(pro_act_dt, 1)
            V.tensor_tensor(sm[:, 9], sm[:, 7], sm[:, 1], ALU.mult).then_inc(pro_dve_a, 1)
            link(V.tensor_tensor(sm[:, 11], sm[:, 8], sm[:, 1], ALU.mult))
            link(V.tensor_scalar(sm[:, 12], sm[:, 11], 1.0 / TWO_PI, MAGIC, ALU.mult, ALU.add))
            link(V.tensor_scalar(sm[:, 13], sm[:, 12], MAGIC, None, ALU.subtract))
            link(V.scalar_tensor_tensor(sm[:, 14], sm[:, 13], -PI_A, sm[:, 11], ALU.mult, ALU.add))
            link(V.scalar_tensor_tensor(sm[:, 15], sm[:, 13], -PI_B, sm[:, 14], ALU.mult, ALU.add))
            link(V.scalar_tensor_tensor(sm[:, 14], sm[:, 13], -PI_C, sm[:, 15], ALU.mult, ALU.add))
            link(V.tensor_scalar(sm[:, 10], sm[:, 14], PI_MAX, -PI_MAX, ALU.min, ALU.max))
            link(V.scalar_tensor_tensor(sm[:, 15], sm[:, 10], -1.0, sm[:, 10], ALU.mult, ALU.max))
            V.tensor_scalar(sm[:, 6], sm[:, 15], -1.0, math.pi / 2, ALU.mult, ALU.add).then_inc(pro_dve_a, 1)
            dve.wait_ge(pro_act_dt, 2)
            V.tensor_scalar(sm[:, 16], sm[:, 4], nsgn, None, ALU.mult).then_inc(w_phasor, 1)
            V.tensor_tensor(P1[:, 1], sm[:, 2], sm[:, 5], ALU.mult)
            V.tensor_tensor(sm[:, 17], sm[:, 2], sm[:, 4], ALU.mult)
            link(V.scalar_tensor_tensor(P2[:, 1], sm[:, 4], nsgn, sm[:, 2], ALU.mult, ALU.mult))
            ts = [tmpE[:, k * 4 * G:(k + 1) * 4 * G] for k in range(4)]
            for a, b, o, n in ((1, 1, 2, 1), (1, 2, 3, 2), (1, 4, 5, 4)):
                bc = lambda t: t[:, b:b + 1].broadcast_to([P, n, G])
                cmul(V, link, (P1[:, o:o + n], P2[:, o:o + n]), (P1[:, a:a + n], P2[:, a:a + n]),
                     (bc(P1), bc(P2)), [x[:, 0:n * G].rearrange("p (n g) -> p n g", n=n) for x in ts])
            lr, li, are, aim = sm[:, 7], sm[:, 8], P1[:, 1], sm[:, 17]
            V.tensor_tensor(sm[:, 18], lr, lr, ALU.mult)
            V.tensor_tensor(sm[:, 19], li, li, ALU.mult)
            V.tensor_scalar(sm[:, 20], are, 1.0, None, ALU.subtract).then_inc(powers, 1)
            dve.wait_ge(powers, 1)
            V.tensor_tensor(sm[:, 21], sm[:, 18], sm[:, 19], ALU.add)
            V.tensor_tensor(sm[:, 22], sm[:, 20], lr, ALU.mult)
            V.tensor_tensor(sm[:, 23], aim, li, ALU.mult)
            V.tensor_tensor(sm[:, 24], aim, lr, ALU.mult)
            link(V.tensor_tensor(sm[:, 25], sm[:, 20], li, ALU.mult))
            V.reciprocal(sm[:, 26], sm[:, 21])
            V.tensor_tensor(sm[:, 27], sm[:, 22], sm[:, 23], ALU.add)
            link(V.tensor_tensor(sm[:, 28], sm[:, 24], sm[:, 25], ALU.subtract))
            V.tensor_tensor(sm[:, 29], sm[:, 27], sm[:, 26], ALU.mult)
            link(V.scalar_tensor_tensor(sm[:, 30], sm[:, 28], nsgn, sm[:, 26], ALU.mult, ALU.mult))
            dve.wait_ge(pro_act, 3)
            fre, fim = (sm[:, k].unsqueeze(2).broadcast_to([P, G, GC]) for k in (29, 30))
            sc = [scr[:, k].rearrange("p (g c) -> p g c", g=G) for k in range(4)]
            V.tensor_tensor(sc[0], Bst[:, :, :], fre, ALU.mult)
            V.tensor_tensor(sc[1], Bsw[:, :, :], fim, ALU.mult)
            V.tensor_tensor(sc[2], Bsw[:, :, :], fre, ALU.mult)
            link(V.tensor_tensor(sc[3], Bst[:, :, :], fim, ALU.mult))
            V.tensor_tensor(Bst[:, :, :], sc[0], sc[1], ALU.add)
            V.tensor_tensor(Bsw[:, :, :], sc[2], sc[3], ALU.subtract).then_inc(b_scaled, 1)
            dve.wait_ge(s_x2, 32)
            for j in range(T // 2, T):
                link(V.tensor_tensor_reduce(X2[:, j], X2[:, j], X2[:, j], 1.0, 0.0, ALU.mult, ALU.add,
                                            ssq[:, 0, j:j + 1]))
            dve.wait_ge(act_seq, T // 2)
            V.tensor_scalar(ssq[:, 1], ssq[:, 0], 1.0 / D, EPS, ALU.mult, ALU.add).then_inc(x_ssq, 1)
            dve.wait_ge(x_sqrt, 1)
            V.reciprocal(ssq[:, 0], ssq[:, 2]).then_inc(xr_set, 1)
            V.memset(Kp[:, :, :], 0.0).then_inc(kp_zero, 1)
            V.memset(zin[:, :, 0:1], 0.0)
            link(V.memset(R[:, :, 0:1], 0.0))

            def u_out(b, par):
                dve.wait_ge(u_ps, b + 1)
                if not isinstance(b, int) or b >= 2:
                    dve.wait_ge(y_ps, b - 1)
                V.tensor_tensor(U[:, par].rearrange("p (a g) k -> p a g k", a=2),
                                ps[:, 4:6, 0:4 * NK].rearrange("p a (g k) -> p a g k", g=4),
                                gainJ[:, ds(b * BG, BG)].rearrange("p (a g) -> p a g", a=2).unsqueeze(3)
                                .broadcast_to([P, 2, 4, NK]), ALU.mult).then_inc(u_set, 1)

            def tau_c(t, b, n):
                return (t[:, 0:n, ds(b * BG, BG)].rearrange("p t g -> p g t").unsqueeze(3)
                        .broadcast_to([P, BG, n, GC]))

            def over_tau(q, b, n):
                return q[:, ds(b * BG, BG)].unsqueeze(2).broadcast_to([P, BG, n, GC])

            def output_powers(b, par):
                if not isinstance(b, int) or b >= 2:
                    dve.wait_ge(y_ps, b - 1)
                n = T + 1
                e = E[:, par]
                t = tmpE[:, :].rearrange("p (g t c) -> p g t c", g=BG, t=n)
                V.tensor_tensor(e, tau_c(P1, b, n), over_tau(Q1, b, n), ALU.mult)
                link(V.tensor_tensor(t, tau_c(P2, b, n), over_tau(Q2, b, n), ALU.mult))
                ins = V.tensor_tensor(e, e, t, ALU.add)
                ins.then_inc(e_set, 1)
                dve.wait_ge(e_set, b + 1)

            def rotation(b, par):
                V.tensor_copy(R[:, :, 1:NK], rho[:, ds(b * BG, BG)].unsqueeze(2).broadcast_to([P, BG, NK - 1]))
                dve.wait_ge(t_base, 1)
                o = T2[:, par].rearrange("p g (a b) -> p g a b", b=8)
                t = tmpE[:, 0:576].rearrange("p (g a b) -> p g a b", g=BG, b=8)
                low = lambda x: x[:, ds(b * BG, BG)].unsqueeze(2).broadcast_to([P, BG, 9, 8])
                high = lambda x: x[:, ds(b * BG, BG)].unsqueeze(3).broadcast_to([P, BG, 9, 8])
                V.tensor_tensor(o, low(TA2), high(TB1), ALU.mult)
                link(V.tensor_tensor(t, low(TA1), high(TB2), ALU.mult))
                link(V.tensor_tensor(o, o, t, ALU.add))

            def kernel_diagonal(b):
                dve.wait_ge(k_copied, b + 1)
                k0 = Kp[:, :, 7 * GC:8 * GC]
                d = tmpE[0:GC, 0:P].rearrange("p (g c) -> p g c", g=BG)
                link(V.tensor_tensor(d, ident[0:GC, 0:GC].unsqueeze(1).broadcast_to([GC, BG, GC]),
                                     dT[:, ds(b * BG, BG)].unsqueeze(2).broadcast_to([GC, BG, GC]), ALU.mult))
                V.tensor_tensor(k0, k0, d, ALU.add).then_inc(kp_set, 1)
                dve.wait_ge(kp_set, b + 1)

            def banks(k, w):
                return ps[:, k:k + 2, 0:4 * NK].rearrange("p a (g k) -> p a g k", g=4)[:, :, :, 0:w]

            def by4(t):
                return t.rearrange("p (a g) k -> p a g k", a=2)

            def scan(b, par):
                dve.wait_ge(v_ps, b + 1)
                dve.wait_ge(t1_set, b + 1)
                w = NK - 1
                V.tensor_tensor(by4(rt1[:, :, 0:w]), by4(T1[:, par, :, 1:NK]), banks(2, w), ALU.mult)
                V.tensor_tensor(by4(rt2[:, :, 0:w]), by4(T2[:, par, :, 1:NK]), banks(4, w), ALU.mult).then_inc(v_read, 1)
                dve.wait_ge(v_read, b + 1)
                link(V.tensor_tensor(zin[:, :, 1:NK], rt1[:, :, 0:w], rt2[:, :, 0:w], ALU.subtract))
                flat = lambda t: t.rearrange("p g k -> p (g k)")
                V.tensor_tensor_scan(flat(zst[:, :, :]), flat(R[:, :, :]), flat(zin[:, :, :]), 0.0,
                                     ALU.mult, ALU.add).then_inc(z_scanned, 1)
                dve.wait_ge(z_scanned, b + 1)

            def states(b, par):
                dve.wait_ge(zsw_ps, b + 1)
                if not isinstance(b, int) or b >= 1:
                    dve.wait_ge(y_ps, b)
                V.tensor_tensor(rt1[:, :, :], T1[:, par, :, 0:NK], zst[:, :, :], ALU.mult)
                link(V.tensor_tensor(by4(rt2[:, :, :]), by4(T2[:, par, :, 0:NK]), banks(6, NK), ALU.mult))
                V.tensor_tensor(Sst[:, :, :], rt1[:, :, :], rt2[:, :, :], ALU.add).then_inc(s_set, 1)
                dve.wait_ge(s_set, b + 1)

            def z_rest(b):
                dve.wait_ge(z_hi, b + 1)
                for h in range(2):
                    v = lambda t: t[:, ds(b, 1)].rearrange("p a (k j) -> p (a j) k", j=T)[:, 4 * h:4 * h + 4]
                    ins = V.tensor_tensor(v(actL), ps[:, h, 0:4 * NK].rearrange("p (j k) -> p j k", j=4),
                                          v(actH).bitcast(F32), ALU.subtract)
                ins.then_inc(z_lo, 1)

            u_out(0, 0)
            output_powers(0, 0)
            rotation(0, 0)
            kernel_diagonal(0)

            def step(b, par, more):
                scan(b, par)
                if more:
                    u_out(b + 1, 1 - par)
                    output_powers(b + 1, 1 - par)
                states(b, par)
                if more:
                    kernel_diagonal(b + 1)
                    rotation(b + 1, 1 - par)
                z_rest(b)

            step(0, 0, True)
            step(1, 1, True)
            with dve.Fori(0, 2) as i:
                link.enter(i, 12)
                for par in range(2):
                    step(i * 2 + (par + 2), par, True)
            link.leave(2)
            step(6, 0, True)
            step(7, 1, False)

            def split_gain(i, ct, gain, n):
                dve.wait_ge(hg_hi[i], n)
                V.scalar_tensor_tensor(hgL[:, ds(ct, 1)], hT[:, ds(ct, 1)], PV[:, ds(gain, 1)],
                                       hgH[:, ds(ct, 1)].bitcast(F32), ALU.mult, ALU.subtract).then_inc(hg_lo[i], 1)

            def glu():
                V.memset(acc[:, :], 0.0).then_inc(glu_free, 1)
                with dve.Fori(0, 4) as i:
                    for q in range(2):
                        p = i * 2 + q
                        dve.wait_ge(glu_sig, p + 1)
                        V.scalar_tensor_tensor(span(cv, ALL), ps[:, (4, 0)[q]:(4, 0)[q] + 2, 0:264],
                                               PV[:, ds(i * 2 + (B_GLU + q), 1)], span(cg, ALL),
                                               ALU.add, ALU.mult).then_inc(glu_free, 1)
                        dve.wait_ge(glu_free, p + 2)
                        V.tensor_tensor(hT[:, ds(p, 1)], hT[:, ds(p, 1)], cv[:, :].unsqueeze(1),
                                        ALU.add).then_inc(h_new[0], 1)
                        split_gain(0, p, i * 2 + (GAIN_FFN + q), p + 1)

            def ffn(l, spans, spans_down, t0):
                nu, nd = (U_UP0, U_DN0) if l == 0 else (U_UP1, U_DN1)
                if l == 0:
                    V.memset(u[:, :, 0:2], 0.0)
                dve.wait_ge(stat_sqrt[2 * l], 1)
                V.reciprocal(rstd[:, :], sqt[:, :]).then_inc(up_free[l], 1)
                dve.wait_ge(up_free[l], 1)
                n = L - t0
                uin = [span(u[:, c, 2:2 + L], spans) for c in range(2)]
                c = (cg, cv)
                col = lambda i, k: PV[:, ds(i * 2 + k, 1)]
                with dve.Fori(0, FT // 2) as i:
                    link.enter(i, 6)
                    for q in range(2):
                        dve.wait_ge(w_used, i * 4 + (nu + 2 * q + 2))
                        V.tensor_tensor(uin[0], pspan(2 * q, spans), span(rstd, spans), ALU.mult)
                        V.tensor_tensor(uin[1], pspan(2 * q + 1, spans), span(rstd, spans),
                                        ALU.mult).then_inc(up_free[l], 1)
                        dve.wait_ge(up_free[l], i * 2 + (q + 2))
                        for k in range(2):
                            ins = V.tensor_scalar(c[k][:, t0:], u[:, k, 2 + t0:2 + L],
                                                  col(i, CONV_W + (3 * l + 2) * 2 * FT + k * FT + q),
                                                  col(i, CONV_B + l * 2 * FT + k * FT + q), ALU.mult, ALU.add)
                        link(ins)
                        for j in (1, 0):
                            for k in range(2):
                                ins = V.scalar_tensor_tensor(c[k][:, t0:], u[:, k, t0 + j:L + j],
                                                             col(i, CONV_W + (3 * l + j) * 2 * FT + k * FT + q),
                                                             c[k][:, t0:], ALU.mult, ALU.add)
                                if j == 0 and k == 0:
                                    ins.then_inc(conv_gate[l], 1)
                            link(ins)
                        dve.wait_ge(silu_set[l], i * 2 + (q + 1))
                        V.tensor_tensor(cg[:, t0:], cg[:, t0:], cv[:, t0:], ALU.mult).then_inc(act_set[l], 1)
                        dve.wait_ge(act_hi[l], i * 2 + (q + 1))
                        V.tensor_tensor(actL[:, ds(i * 2 + q, 1), t0:], cg[:, t0:].unsqueeze(1),
                                        actH[:, ds(i * 2 + q, 1), t0:].bitcast(F32), ALU.subtract).then_inc(act_lo[l], 1)
                link.leave(FT // 2)
                if l == 0:
                    with dve.Fori(0, 2) as i:
                        for m in range(4):
                            add_down(l, i * 4 + m, i * 12 + (nd + 3 * m + 3), m, spans_down)
                            split_gain(1, i * 4 + m, i * 4 + (GAIN_MIX + 8 + m), i * 4 + (m + 1))

                else:
                    with dve.Fori(0, 2) as i:
                        link.enter(i, 0)
                        for m in range(4):
                            n = i * 4 + m
                            dve.wait_ge(w_used, i * 12 + (nd + 3 * m + 3))
                            if m >= 2:
                                dve.wait_ge(yt_ps, n - 1)
                            else:
                                dve.wait_ge(yt_ps, i * 4)
                            h = span(hT[:, ds(n, 1)].rearrange("p a t -> p (a t)"), spans_down)
                            V.tensor_tensor((cg, cv)[m % 2][:, 0:SEQ].rearrange("p (a b) -> p a b", a=2), h,
                                            pspan(m % 2, spans_down), ALU.add).then_inc(h_new[3], 1)
                            if m:
                                y_turned(i * 4 + (m - 1), m - 1)
                        y_turned(i * 4 + 3, 3)
                    link.leave(2)
                    dve.wait_ge(y_sqs, 4 * CT)
                    V.tensor_reduce(ytot, ysum.rearrange("p (n t) -> p t n", t=4), AX.X, ALU.add).then_inc(y_set, 1)
                    dve.wait_ge(y_root, 1)
                    link(V.reciprocal(yinv, yrt))
                    dve.wait_ge(y_set, CT + 1)
                    for t in range(SEQ // P):
                        V.tensor_scalar(ytok[:, t], ytok[:, t], yinv[:, t:t + 1], None, ALU.mult).then_inc(y_out, 1)

            def y_turned(n, m):
                if m == 0:
                    dve.wait_ge(fgain_in, 16)
                dve.wait_ge(yt_ps, n + 1)
                V.tensor_tensor(ytok[:, :, ds(n * P, P)], ps[:, 4 + m % 2].rearrange("p (t c) -> p t c", c=P),
                                fgain[:, ds(n * P, P)].unsqueeze(1).broadcast_to([P, SEQ // P, P]),
                                ALU.mult).then_inc(y_set, 1)

            def qkv():
                dve.wait_ge(stat_sqrt[1], 1)
                dve.wait_ge(cs_in, 16)
                link(V.reciprocal(rstd[:, :], sqt[:, :]))
                V.tensor_tensor(cs[:, :], cs[:, :], rstd[:, :].unsqueeze(1).broadcast_to([P, 2, L]),
                                ALU.mult).then_inc(qk_set, 1)
                dve.wait_ge(qk_set, 1)
                with dve.Fori(0, 4) as i:
                    link.enter(i, 4)
                    for m in range(4):
                        dve.wait_ge(rope_sw, i * 4 + (m + 1))
                        V.tensor_tensor(span(cv, ALL), pspan(m % 2, ALL), span(cs[:, 0], ALL), ALU.mult)
                        link(V.tensor_tensor(cg[:, :], cg[:, :], cs[:, 1], ALU.mult))
                        V.tensor_tensor(qk[:, ds(i * 4 + m, 1)], cv[:, :].unsqueeze(1), cg[:, :].unsqueeze(1),
                                        ALU.add).then_inc(qk_set, 1)
                link.leave(4)
                with dve.Fori(0, 2) as i:
                    for m in range(4):
                        dve.wait_ge(w_used, i * 4 + (U_QKV + 17 + m))
                        dve.wait_ge(v_turned, i * 4 + (m - 1) if m >= 2 else i * 4)
                        V.tensor_tensor(span((cg, cv)[m % 2], ALL), pspan(m % 2, ALL), span(rstd, ALL),
                                        ALU.mult).then_inc(v_norm, 1)

            def maxima(n, i):
                nq = TILES[i][1]
                nk = sum(TILES[i])
                for c in range(2):
                    dve.wait_ge(sc_ps, n * 2 + (c + 1))
                    link(V.tensor_reduce(mx[0:nq, c:c + 1], score_row(c, nq, nk), AX.X, ALU.max))
                    V.tensor_scalar(nm[0:nq, c:c + 1], mx[0:nq, c:c + 1], -SCALE, None, ALU.mult).then_inc(max_set, 1)

            def difference(n, i):
                nq = TILES[i][1]
                nk = sum(TILES[i])
                dve.wait_ge(probs_set, n * 2 + 2)
                if not isinstance(n, int) or n:
                    dve.wait_ge(pt_ps, n)
                link(V.reciprocal(inv[0:nq, i], esum[0:nq]))
                link(V.tensor_scalar(ratio[0:nq], esum[0:nq, 0:1], inv[0:nq, i, 1:2], nlam[0:nq], ALU.mult, ALU.mult))
                V.scalar_tensor_tensor(Ab[0:nq, 0:nk], Pb[0:nq, 1, 0:nk], ratio[0:nq], Pb[0:nq, 0, 0:nk],
                                       ALU.mult, ALU.add).then_inc(diff_set, 1)

            def attend(h, n, i, first=False, last=False):
                nq = TILES[i][1]
                more = not (last and i == NT - 1)
                if more:
                    maxima(n + 1, (i + 1) % NT)
                dve.wait_ge(pt_ps, n + 1)
                dve.wait_ge(o_ps, n)
                if i:
                    V.tensor_copy(AT[:, 1:i + 1], ps[:, 4].rearrange("p (t q) -> p t q", q=P)[:, 0:i])
                V.tensor_copy(AT[0:META, 0], ps[0:META, 5, 0:P]).then_inc(at_set, 1)
                if more:
                    difference(n + 1, (i + 1) % NT)
                if i == 0 and not first:
                    head_norm(h - 1)
                dve.wait_ge(o_ps, n + 1)
                dve.wait_ge(o_sq, n)
                V.tensor_scalar(Ob[0:nq, i], ps[0:nq, 5, P:2 * P], inv[0:nq, i, 0:1], None, ALU.mult).then_inc(o_set, 1)
                if i == 2 and not first:
                    head_rest(h - 1)

            def head_norm(h):
                dve.wait_ge(sub_root, h + 1)
                dve.wait_ge(o_set, (h + 1) * NT)
                dve.wait_ge(ot_ps, h)
                link(V.reciprocal(hinv, hrt))
                V.tensor_scalar(On[0:META, 0], Ob[0:META, 0], hinv[0:META, 0:1], None, ALU.mult)
                V.tensor_tensor(On[:, 1:NT], Ob[:, 1:NT], hinv[:, 1:NT].unsqueeze(2).broadcast_to([P, NT - 1, P]),
                                ALU.mult).then_inc(on_set, 1)
                dve.wait_ge(on_set, h + 1)

            def head_rest(h):
                dve.wait_ge(o_hi, h + 1)
                V.scalar_tensor_tensor(oL[:, ds(h, 1)], turned_row.unsqueeze(1), sub_gain,
                                       oH[:, ds(h, 1)].bitcast(F32), ALU.mult, ALU.subtract).then_inc(o_lo, 1)

            def attention():
                dve.wait_ge(lam_exp, 1)
                link(V.tensor_tensor(nlam, lam_e[:, 1:2], lam_e[:, 0:1], ALU.subtract))
                link(V.tensor_scalar(nlam, nlam, LAMBDA_INIT, None, ALU.subtract))
                V.memset(hsq, 1.0)
                link(V.tensor_scalar(sub_gain, PV[:, SUBLN:SUBLN + 1], 1.0 - LAMBDA_INIT, None, ALU.mult))
                dve.wait_ge(w_used, U_WO)
                V.memset(Ab[:, 0:META], 0.0)
                link(V.memset(AT[:, 0], 0.0))
                maxima(0, 0)
                difference(0, 0)
                for i in range(NT):
                    attend(0, i, i, first=True)
                with dve.Fori(0, HEADS - 2) as h:
                    link.enter(h, 4 * NT + 1)
                    for i in range(NT):
                        attend(h + 1, h * NT + (NT + i), i)
                link.leave(HEADS - 2)
                for i in range(NT):
                    attend(HEADS - 1, (HEADS - 1) * NT + i, i, last=True)
                head_norm(HEADS - 1)
                head_rest(HEADS - 1)

            def out_projection():
                with dve.Fori(0, 2) as i:
                    for m in range(4):
                        n = i * 4 + m
                        dve.wait_ge(w_used, n + (U_WO + 1))
                        V.tensor_tensor(span(hT[:, ds(n, 1)].rearrange("p a t -> p (a t)"), ALL),
                                        span(hT[:, ds(n, 1)].rearrange("p a t -> p (a t)"), ALL),
                                        pspan(m % 2, ALL), ALU.add).then_inc(h_new[2], 1)
                        split_gain(2, n, i * 4 + (GAIN_FFN + 8 + m), n + 1)

            def add_down(l, ct, used, m, spans):
                dve.wait_ge(w_used, used)
                h = span(hT[:, ds(ct, 1)].rearrange("p a t -> p (a t)"), spans)
                V.tensor_tensor(h, h, pspan(m % 2, spans), ALU.add).then_inc(h_new[1 + 2 * l], 1)

            glu()
            ffn(0, ALL, ALL, 0)
            dve.wait_ge(lam_in, 16)
            t = tiny[:, 384:512].rearrange("p (a b) -> p a b", a=2)
            l4 = lam.rearrange("p (a c b) -> p a c b", a=2, c=2)
            link(V.tensor_tensor(t, l4[:, :, 0], l4[:, :, 1], ALU.mult))
            V.tensor_reduce(lam_s, t, AX.X, ALU.add).then_inc(lam_sum, 1)
            qkv()
            attention()
            out_projection()
            ffn(1, FROM12, FROM16, META)

        @block.gpsimd
        def _(pool):
            V = nc.gpsimd
            link = Chain(pool, pool_seq)

            def cmul(o, a, b, t):
                V.tensor_tensor(t[0], a[0], b[0], ALU.mult)
                V.tensor_tensor(t[1], a[1], b[1], ALU.mult)
                V.tensor_tensor(t[2], a[1], b[0], ALU.mult)
                link(V.tensor_tensor(t[3], a[0], b[1], ALU.mult))
                V.tensor_tensor(o[0], t[0], t[1], ALU.subtract)
                link(V.tensor_tensor(o[1], t[2], t[3], ALU.add))

            tp = [tmpP[:, k * 256:(k + 1) * 256] for k in range(4)]
            small = [t[:, 0:G] for t in tp]
            pool.wait_ge(w_phasor, 1)
            w1, w2 = sm[:, 5], sm[:, 16]
            phasors = {1: (w1, w2)}
            for k, n in enumerate((2, 4, 8, 16, 32, 64, 128, 256, 512)):
                o = (pw[:, 2 * k], pw[:, 2 * k + 1])
                cmul(o, phasors[n // 2], phasors[n // 2], small)
                phasors[n] = o
            V.memset(TA1[:, :, 0:1], 1.0)
            V.memset(TA2[:, :, 0:1], 0.0)
            V.memset(TB1[:, :, 0:1], 1.0)
            link(V.memset(TB2[:, :, 0:1], 0.0))
            for (t1, t2), first in (((TA1, TA2), 8), ((TB1, TB2), 64)):
                for n in (1, 2, 4) + ((8,) if first == 64 else ()):
                    w = phasors[first * n]
                    m = n if n < 8 else 1
                    cmul((t1[:, :, n:n + m], t2[:, :, n:n + m]), (t1[:, :, 0:m], t2[:, :, 0:m]),
                         [x.unsqueeze(2).broadcast_to([P, G, m]) for x in w],
                         [x[:, 0:G * m].rearrange("p (g n) -> p g n", g=G) for x in tp])
            pool.wait_ge(powers, 1)
            V.tensor_copy(PR1[:, 0], P1[:, T - 1]).then_inc(t_base, 1)
            V.tensor_copy(PR2[:, 0], P2[:, T - 1])
            for j in range(1, T):
                V.tensor_copy(PR1[:, j], P1[:, T - 1 - j])
                ins = V.tensor_copy(PR2[:, j], P2[:, T - 1 - j])
            link(ins)
            for n in range(2):
                split_lo(pool, n, n)

            def normed(b, par):
                pool.wait_ge(xb_in[par], (b - par) * 16 + 32)
                if not isinstance(b, int) or b >= 1:
                    pool.wait_ge(u_ps, b)
                V.tensor_tensor(xn[:, :], xb[:, par].rearrange("k j (g c) -> k g j c", c=GC),
                                ssq[:, 0].unsqueeze(1).unsqueeze(3).broadcast_to([NK, BG, T, GC]), ALU.mult).then_inc(xn_set, 1)

            def input_powers(b):
                if not isinstance(b, int) or b >= 1:
                    pool.wait_ge(k_ps, b)
                over = lambda t: t[:, ds(b * BG, BG)].unsqueeze(2).broadcast_to([P, BG, T, GC])
                at_j = lambda t: (t[:, :, ds(b * BG, BG)].rearrange("p j g -> p g j").unsqueeze(3)
                                  .broadcast_to([P, BG, T, GC]))
                t = tmpP[:, :].rearrange("p (g j c) -> p g j c", g=BG, j=T)
                V.tensor_tensor(F[:, :], at_j(PR1), over(Bst), ALU.mult)
                link(V.tensor_tensor(t, at_j(PR2), over(Bsw), ALU.mult))
                V.tensor_tensor(F[:, :], F[:, :], t, ALU.add).then_inc(f_set, 1)
                pool.wait_ge(f_set, b + 1)

            def rotation(b, par):
                if not isinstance(b, int) or b >= 2:
                    pool.wait_ge(s_set, b - 1)
                o = T1[:, par].rearrange("p g (a b) -> p g a b", b=8)
                t = tmpP[:, 0:576].rearrange("p (g a b) -> p g a b", g=BG, b=8)
                low = lambda x: x[:, ds(b * BG, BG)].unsqueeze(2).broadcast_to([P, BG, 9, 8])
                high = lambda x: x[:, ds(b * BG, BG)].unsqueeze(3).broadcast_to([P, BG, 9, 8])
                V.tensor_tensor(o, low(TA1), high(TB1), ALU.mult)
                link(V.tensor_tensor(t, low(TA2), high(TB2), ALU.mult))
                V.tensor_tensor(o, o, t, ALU.subtract).then_inc(t1_set, 1)
                pool.wait_ge(t1_set, b + 1)

            pool.wait_ge(b_scaled, 1)
            input_powers(0)
            rotation(0, 0)
            pool.wait_ge(xr_set, 1)
            normed(0, 0)
            normed(1, 1)
            input_powers(1)
            rotation(1, 1)
            with pool.Fori(0, 3) as i:
                link.enter(i, 4)
                for par in range(2):
                    b = i * 2 + (par + 2)
                    normed(b, par)
                    input_powers(b)
                    rotation(b, par)
            link.leave(3)

            def square(i, ct, n):
                pool.wait_ge(h_new[i], n)
                link(V.tensor_tensor(sqt[:, :].unsqueeze(1), hT[:, ds(ct, 1)], hT[:, ds(ct, 1)], ALU.mult))
                V.tensor_tensor(acc[:, :], acc[:, :], sqt[:, :], ALU.add).then_inc(sq_sum[i], 1)
                pool.wait_ge(sq_sum[i], n)

            def glu():
                for n in (2, 3):
                    split_lo(pool, n, n)
                pool.wait_ge(glu_free, 1)
                with pool.Fori(0, 4) as i:
                    link.enter(i, 2)
                    for q in range(2):
                        for c in range(2):
                            split_lo(pool, i * 4 + (4 + 2 * q + c), 2 * q + c)
                        square(0, i * 2 + q, i * 2 + (q + 1))
                link.leave(4)

            def ffn(l):
                nu, nd = (U_UP0, U_DN0) if l == 0 else (U_UP1, U_DN1)
                if l == 0:
                    clear_sum(0)
                with pool.Fori(0, FT // 2) as i:
                    for c in range(4):
                        split_lo(pool, i * 4 + (nu + 4 + c), c)
                if l == 0:
                    with pool.Fori(0, 2) as i:
                        link.enter(i, 4)
                        for m in range(4):
                            for kc in range(3):
                                c = 3 * m + kc
                                split_lo(pool, i * 12 + (nd + 4 + c), c % 4, (8, 8, 6)[(c + 4) % 3] if c < 8 else 8)
                            square(1, i * 4 + m, i * 4 + (m + 1))
                    link.leave(2)

                if l == 1:
                    for c in range(20):
                        split_lo(pool, nd + 4 + c, c % 4, (8, 8, 6)[(c + 4) % 3])

            def clear_sum(i):
                pool.wait_ge(stat_ps[i], 1)
                link(V.memset(acc[:, :], 0.0))

            def qkv():
                clear_sum(1)
                pool.wait_ge(w_used, U_QKV)
                V.memset(vtok[:, 0], 0.0).then_inc(v_zero, 1)
                with pool.Fori(0, 6) as i:
                    for c in range(4):
                        split_lo(pool, i * 4 + (U_QKV + 4 + c), c)

            def attention():
                pool.wait_ge(w_used, U_WO)
                pool.wait_ge(qk_set, 2 * HEADS + 1)
                V.tensor_copy(qs[:, :], qk[:, 0])
                V.tensor_copy(ks[:, :], qk[:, HEADS]).then_inc(head_in, 1)
                with pool.Fori(0, HEADS - 1) as h:
                    pool.wait_ge(sc_ps, h * (2 * NT) + 2 * NT)
                    V.tensor_copy(qs[:, :].unsqueeze(1), qk[:, ds(h + 1, 1)])
                    V.tensor_copy(ks[:, :].unsqueeze(1), qk[:, ds(h + (HEADS + 1), 1)]).then_inc(head_in, 1)

            def out_projection():
                with pool.Fori(0, 2) as i:
                    link.enter(i, 4)
                    for m in range(4):
                        split_lo(pool, i * 4 + (U_WO + 4 + m), m)
                        square(2, i * 4 + m, i * 4 + (m + 1))
                link.leave(2)

            glu()
            ffn(0)
            qkv()
            attention()
            out_projection()
            ffn(1)


_INS = ["x", "meta_tokens", "norm_mix_gain", "norm_ffn_gain", "s5_a_re", "s5_a_im", "s5_log_dt", "s5_b_re", "s5_b_im",
        "s5_c_re", "s5_c_im", "s5_d", "s5_w_glu", "s5_b_glu", "attn_w_qkv", "attn_lambda", "attn_subln_gain",
        "attn_w_o", "ffn_w_up", "ffn_conv_w", "ffn_conv_b", "ffn_w_down", "final_norm_gain"]


def kernel(**inputs):
    import concourse.bacc as bacc
    from concourse.bass_utils import run_bass_kernel_spmd

    nc = bacc.Bacc("TRN2", target_bir_lowering=False, num_devices=1)
    arrays = {n: np.ascontiguousarray(inputs[n]) for n in _INS}
    aps = {n: nc.dram_tensor(n, a.shape, mybir.dt.from_np(a.dtype), kind="ExternalInput").ap()
           for n, a in arrays.items()}
    out = nc.dram_tensor("out", (1, SEQ, D), F32, kind="ExternalOutput").ap()
    build(nc, aps, out)
    r = run_bass_kernel_spmd(nc, [arrays], core_ids=[0])
    return r.results[0]["out"]
```

```python
import math
from contextlib import ExitStack

import numpy as np
import concourse.bass as bass
from concourse import mybir

F32 = mybir.dt.float32
F32R = mybir.dt.float32r
ACT = mybir.ActivationFunctionType
ALU = mybir.AluOpType
AX = mybir.AxisListType

P = 128
D = 1024
CT = D // P
META = 16
SEQ = 512
L = META + SEQ
FF = 2816
FT = FF // P
EPS = 1e-6
G, NST, GC = 64, 64, 16
T = 8
NK = L // T
BG = P // GC
HEADS, HD = 8, 64
LAMBDA_INIT = 0.8 - 0.6 * math.exp(-0.3 * 1)

CONV_W, CONV_B, GAIN_MIX, GAIN_FFN, B_GLU, SUBLN = 0, 264, 352, 368, 384, 400
PV_COLS = 401

U_GLU, U_UP0, U_DN0, U_QKV, U_WO, U_UP1, U_DN1, U_END = 0, 16, 60, 84, 108, 116, 160, 184

ALL = ((0, 264), (264, 264))
FROM12 = ((12, 258), (270, 258))
FROM16 = ((16, 256), (272, 256))

TILES = ((0, META),) + tuple((META + P * i, P) for i in range(SEQ // P))
NT = len(TILES)
NQ = NT - 1
CUT = META + 2 * P
PS_COL = 512 - CUT
SCALE = HD ** -0.5

WORDS0 = 16512
MAGIC = 1.5 * 2.0 ** 23
TWO_PI = 2.0 * math.pi
PI_A = 6.28125
PI_B = float(np.float32(round((TWO_PI - PI_A) * 2 ** 21) / 2 ** 21))
PI_C = float(np.float32(TWO_PI - PI_A - PI_B))
PI_MAX = 3.1415925

FREE = 1


def shape_constants():
    eye = np.eye(P, dtype=np.float32)
    swap64 = np.roll(eye, 64, axis=0)
    swap32 = np.zeros((P, P), np.float32)
    for p in range(P):
        swap32[p ^ 32, p] = 1.0
    q, k = np.arange(P)[:, None], np.arange(P)[None, :]
    mask = np.where(k <= q, 0.0, -(2.0 ** 100)).astype(np.float32)
    sign = np.where(np.arange(P) < 64, 1.0, -1.0).astype(np.float32)[:, None]
    half = HD // 2
    inv = (10000.0 ** (-np.arange(half, dtype=np.float32) / np.float32(half))).astype(np.float32)
    ang = (np.arange(L, dtype=np.float32)[None, :] * inv[:, None]).astype(np.float32)
    cos = np.tile(np.cos(ang), (4, 1)).astype(np.float32)
    sin = np.tile(np.concatenate([-np.sin(ang), np.sin(ang)]), (2, 1)).astype(np.float32)
    return np.concatenate([eye, swap64, swap32, mask, sign, -sign, cos, sin], axis=1)


class Chain:

    def __init__(self, eng, sem):
        self.eng, self.sem, self.base, self.k = eng, sem, 0, 0

    def __call__(self, ins):
        ins.then_inc(self.sem, 1)
        self.k += 1
        self.eng.wait_ge(self.sem, self.base + self.k)

    def enter(self, i, steps):
        self.start, self.steps = self.base + self.k, steps
        self.base, self.k = i * steps + self.start, 0

    def leave(self, rounds):
        assert self.k == self.steps, (self.k, self.steps)
        self.base, self.k = self.start + rounds * self.steps, 0


def build(nc, inp, out):
    ds = bass.ds
    consts = nc.inline_tensor(shape_constants(), name="shape_constants").ap()
    ctx = ExitStack()
    with ctx:
        def sem(name):
            return ctx.enter_context(nc.semaphore(name))

        top = [0]

        def at(name, shape, dt, offset=None):
            words = int(np.prod(shape[1:]))
            o = top[0] if offset is None else offset
            if offset is None:
                top[0] += -(-words // 8) * 8
            return nc.alloc_sbuf_tensor_at(name, list(shape), dt, offset=WORDS0 + 4 * o)

        hT = at("hT", [P, CT, L], F32)
        O_HG = top[0]
        hgH = at("hgH", [P, CT, L], F32R)
        hgL = at("hgL", [P, CT, L], F32R)
        O_ACTH = top[0]
        actH = at("actH", [P, FT, L], F32R)
        O_ACTL = top[0]
        actL = at("actL", [P, FT, L], F32R)
        raw = at("raw", [P, 2, 8, P], F32)
        wH = at("wH", [P, 4, 8, P], F32R)
        O_WL = top[0]
        wL = at("wL", [P, 4, 8, P], F32R)
        O_WH = O_WL - 4096
        cst = at("cst", [P, 514], F32)
        PV = at("PV", [P, PV_COLS], F32)
        O_SCR = top[0]
        ones = at("ones", [P, P], F32)
        rstd = at("rstd", [P, L], F32)
        acc = at("acc", [P, L], F32)
        sqt = at("sqt", [P, L], F32)
        u = at("u", [P, 2, L + 2], F32)
        cg = at("cg", [P, L], F32)
        cv = at("cv", [P, L], F32)
        vstage = at("vstage", [P, 4, P], F32)
        tiny = at("tiny", [P, 640], F32)
        O_SPARE = top[0]
        cs = at("cs", [P, 2, L], F32, offset=O_SPARE)
        fgain = at("fgain", [P, D], F32, offset=O_SPARE)

        qk = at("qk", [P, 2 * HEADS, L], F32, offset=O_ACTH)
        vtok = at("vtok", [P, NT, D], F32, offset=O_ACTH + 2 * HEADS * L)
        O_OT = O_ACTH + 2 * HEADS * L + NT * D
        oH = at("oH", [P, CT, L], F32R, offset=O_OT)
        oL = at("oL", [P, CT, L], F32R, offset=O_OT + CT * L)
        assert O_OT + 2 * CT * L <= O_ACTL + FT * L
        o_att = [O_HG]

        def att(name, shape, dt=F32):
            t = at(name, shape, dt, offset=o_att[0])
            words = int(np.prod(shape[1:])) * mybir.dt.size(dt) // 4
            o_att[0] += -(-words // 8) * 8
            assert o_att[0] <= O_ACTH or O_OT < o_att[0] <= O_ACTL + FT * L
            return t

        Pb = att("Pb", [P, 2, L])
        Ab = att("Ab", [P, L])
        AT = att("AT", [P, NT, P])
        Ob = att("Ob", [P, 2, NQ, P])
        On = att("On", [P, NQ, P])
        S0 = att("S0", [META, 2, HEADS, META])
        P0 = att("P0", [META, 2, HEADS, META])
        A0 = att("A0", [META, HEADS, META])
        AT0 = att("AT0", [META, HEADS, META])
        O0 = att("O0", [META, HEADS, P])
        ON0 = att("ON0", [META, HEADS, P])
        f0 = att("f0", [META, 128])
        o_hg = o_att[0]
        o_att[0] = O_OT + 2 * CT * L
        qs = att("qs", [P, L])
        ks = att("ks", [P, L])
        identB = att("identB", [P, P], mybir.dt.bfloat16)
        maskB = att("maskB", [P, P], mybir.dt.bfloat16)
        o_att[0] = o_hg
        osq = att("osq", [P, P])
        ytok = at("ytok", [P, SEQ // P, D], F32, offset=O_HG)
        ysq = at("ysq", [P, P], F32, offset=O_HG + 4 * D)
        END = (229344 - WORDS0) // 4
        assert top[0] <= END, (top[0], END)

        ident, swap64, swap32, mask = (cst[:, i * P:(i + 1) * P] for i in range(4))
        sgn, nsgn = cst[:, 512:513], cst[:, 513:514]

        ps = ctx.enter_context(nc.psum_tensor("ps", [P, 8, 512], F32))

        def pspan(slot, spans):
            return ps[:, 2 * slot:2 * slot + 2, 0:spans[0][1]]

        def span(ap, spans):
            t0, w = spans[0]
            return ap[:, t0:t0 + 2 * w].rearrange("p (a b) -> p a b", a=2)

        def score_row(c, nq, nk):
            return ps[0:nq, 2 * c:2 * c + 2].rearrange("p a b -> p (a b)")[:, PS_COL:PS_COL + nk]

        turned_row = ps[:, 7:8, :]

        first_row = ps[:, 7, 0:HEADS * META].rearrange("p (h q) -> p h q", q=META)

        raw_in = [sem(f"raw_in{i}") for i in range(2)]
        w_hi = sem("w_hi")
        w_lo = sem("w_lo")
        w_used = sem("w_used")

        glu_w = inp["s5_w_glu"]
        qkv_w, wo_w = inp["attn_w_qkv"], inp["attn_w_o"]
        up_w, down_w = inp["ffn_w_up"], inp["ffn_w_down"]

        def cols(mat, c0, r0=0, nk=8):
            return mat[r0:r0 + nk * P, ds(c0, P)].rearrange("(k p) c -> p k c", p=P)

        def load_unit(sp, n, src, slot, nk=8):
            if not isinstance(n, int) or n >= 2:
                sp.wait_ge(w_lo, n - 1)
            sp.dma_start(raw[:, slot % 2, 0:nk, :], src).then_inc(raw_in[slot % 2], 16)

        def split_hi(act, n, slot, half, nk=8):
            act.wait_ge(raw_in[slot % 2], half * 16 + 16)
            if not isinstance(n, int) or n >= 4:
                act.wait_ge(w_used, n - 3)
            nc.scalar.activation(wH[:, slot, 0:nk], raw[:, slot % 2, 0:nk], ACT.Copy).then_inc(w_hi, 1)

        def split_lo(pool, n, slot, nk=8):
            pool.wait_ge(w_hi, n + 1)
            nc.gpsimd.tensor_tensor(wL[:, slot, 0:nk], raw[:, slot % 2, 0:nk], wH[:, slot, 0:nk].bitcast(F32),
                                    ALU.subtract).then_inc(w_lo, 1)

        def unit_products(pe, n, slot, bank, xH, xL, spans, kt0, nk, first, last, ready=None):
            pe.wait_ge(w_hi, n + 1)
            pe.wait_ge(w_lo, n + 1)
            for k in range(nk):
                kt = kt0 + k
                if ready is not None:
                    ready(kt)
                for w, x, s0, s1 in ((wH, xH, True, False), (wH, xL, False, False), (wL, xH, False, True)):
                    for b, (t0, tw) in enumerate(spans):
                        mm = nc.tensor.matmul(ps[:, bank + b, 0:tw], w[:, slot, k, :], x[:, kt, t0:t0 + tw],
                                              start=first and k == 0 and s0,
                                              stop=last and k == nk - 1 and s1)
            mm.then_inc(w_used, 1)

        O = [O_HG]

        def s5(name, shape, dt=F32):
            words = -(-int(np.prod(shape[1:])) // 8) * 8
            for r in regions:
                if r[1] - r[0] >= words:
                    o = r[0]
                    r[0] += words
                    return nc.alloc_sbuf_tensor_at(name, list(shape), dt, offset=WORDS0 + 4 * o)
            raise AssertionError((name, words, regions))

        regions = [[O_HG, O_ACTH], [O_ACTH + CT * L, O_ACTL], [O_ACTL + CT * L, O_ACTL + FT * L],
                   [O_WH + 2048, O_WH + 4096], [O_WL + 2048, O_WL + 4096], [O_SPARE, END],
                   [O_SCR + 128, O_SCR + 128 + 3 * L + 2 * (L + 2) + 2 * L - 8]]
        o_x2 = regions[0][0]
        X2 = at("X2", [NK, T, D], F32, offset=o_x2)
        TT = s5("TT", [P, 2, BG, P])
        Kp = s5("Kp", [GC, BG, 15 * GC])
        Z2 = s5("Z2", [NK, T, P])
        rt1 = s5("rt1", [P, BG, NK])
        rt2 = s5("rt2", [P, BG, NK])
        zin = s5("zin", [P, BG, NK])
        zst = s5("zst", [P, BG, NK])
        Sst = s5("Sst", [P, BG, NK])
        assert regions[0][0] - o_x2 <= 8192
        regions[0][0] = max(regions[0][0], o_x2 + 8192)
        o_bn = regions[1][0]
        Bn = at("Bn", [G, 2, D], F32, offset=o_bn)
        Cn = at("Cn", [P, CT, 2, NST], F32, offset=o_bn + 2048)
        E = s5("E", [P, 2, BG, T + 1, GC])
        F = s5("F", [P, BG, T, GC])
        assert regions[1][0] - o_bn >= 3072
        Bst = s5("Bst", [P, G, GC])
        Bsw = s5("Bsw", [P, G, GC])
        Q1 = s5("Q1", [P, G, GC])
        Q2 = s5("Q2", [P, G, GC])
        WBT = s5("WBT", [P, BG, P])
        xb = s5("xb", [NK, 2, T, P])
        xn = s5("xn", [NK, BG, T, GC])
        U = s5("U", [P, 2, BG, NK])
        P1 = s5("P1", [P, T + 1, G])
        P2 = s5("P2", [P, T + 1, G])
        PR1 = s5("PR1", [P, T, G])
        PR2 = s5("PR2", [P, T, G])
        TA1 = s5("TA1", [P, G, 8])
        TA2 = s5("TA2", [P, G, 8])
        TB1 = s5("TB1", [P, G, 9])
        TB2 = s5("TB2", [P, G, 9])
        T1 = s5("T1", [P, 2, BG, 72])
        T2 = s5("T2", [P, 2, BG, 72])
        R = s5("R", [P, BG, NK])
        tmpE = s5("tmpE", [P, 1152])
        tmpP = s5("tmpP", [P, 1024])
        gainJ = s5("gainJ", [P, G])
        dT = s5("dT", [GC, G])
        an = s5("an", [G, 2, 2, NST])
        gd = s5("gd", [G, T + 1, GC])
        rho = s5("rho", [P, G])
        ssq = s5("ssq", [NK, 3, T])
        scr = at("scr", [P, 4, D], F32, offset=O_ACTL)
        junk = at("junk", [P, D], F32, offset=O_ACTH)
        pw = at("pw", [P, 18, G], F32, offset=O_ACTH + D)
        sm = at("sm", [P, 32, G], F32, offset=O_ACTH + D + 18 * G)
        eps_col = tiny[:, 0:1]
        nlam = tiny[:, 1:2]
        lam_s = tiny[:, 2:4]
        lam_e = tiny[:, 4:6]
        mx, nm, esum = tiny[:, 8:10], tiny[:, 10:12], tiny[:, 12:14]
        ratio = tiny[:, 14:15]
        inv = tiny[:, 16:24].rearrange("p (i c) -> p i c", c=2)
        hsq, hrt, hinv = (tiny[:, 32:36], tiny[:, 24:28]), tiny[:, 40:44], tiny[:, 48:52]
        by_c = lambda t: t.rearrange("p (c h) -> p c h", c=2)
        mx0, sum0, inv0 = by_c(f0[:, 0:16]), by_c(f0[:, 16:32]), by_c(f0[:, 32:48])
        ratio0, sq0, rt0, rinv0 = (f0[:, k:k + 8] for k in (48, 56, 64, 72))
        sub_gain = tiny[:, 56:57]
        ysum = tiny[:, 64:96]
        ytot, yrt, yinv = tiny[:, 96:100], tiny[:, 100:104], tiny[:, 104:108]
        lam = tiny[:, 128:384]

        s_const = sem("s_const")
        s_x2 = sem("s_x2")
        s_an = sem("s_an")
        s_bn = sem("s_bn")
        s_cn = sem("s_cn")
        s_vec = sem("s_vec")
        s_dt = sem("s_dt")
        ones_set = sem("ones_set")
        pro_ps = sem("pro_ps")
        pro_act = sem("pro_act")
        dve_seq = sem("dve_seq")
        pool_seq = sem("pool_seq")
        act_seq = sem("act_seq")
        xb_in = [sem(f"xb_in{i}") for i in range(2)]
        xn_set = sem("xn_set")
        xt_ps = sem("xt_ps")
        xt_out = sem("xt_out")
        u_ps = sem("u_ps")
        u_set = sem("u_set")
        f_set = sem("f_set")
        ft_ps = sem("ft_ps")
        wbt_set = sem("wbt_set")
        e_set = sem("e_set")
        k_ps = sem("k_ps")
        k_copied = sem("k_copied")
        kp_set = sem("kp_set")
        tt_in = [sem(f"tt_in{i}") for i in range(2)]
        v_ps = sem("v_ps")
        v_read = sem("v_read")
        z_scanned = sem("z_scanned")
        zsw_ps = sem("zsw_ps")
        s_set = sem("s_set")
        y_ps = sem("y_ps")
        gelu_set = sem("gelu_set")
        zt_ps = sem("zt_ps")
        z_hi = sem("z_hi")
        z_lo = sem("z_lo")
        t1_set = sem("t1_set")

        STAT = (2, 6, 2)

        glu_sig = sem("glu_sig")
        glu_free = sem("glu_free")
        h_new = [sem(f"h_new{i}") for i in range(4)]
        hg_hi = [sem(f"hg_hi{i}") for i in range(3)]
        hg_lo = [sem(f"hg_lo{i}") for i in range(3)]
        sq_sum = [sem(f"sq_sum{i}") for i in range(3)]
        stat_ps = [sem(f"stat_ps{i}") for i in range(3)]
        stat_sqrt = [sem(f"stat_sqrt{i}") for i in range(3)]
        up_free = [sem(f"up_free{i}") for i in range(2)]
        conv_gate = [sem(f"conv_gate{i}") for i in range(2)]
        silu_set = [sem(f"silu_set{i}") for i in range(2)]
        act_set = [sem(f"act_set{i}") for i in range(2)]
        act_hi = [sem(f"act_hi{i}") for i in range(2)]
        act_lo = [sem(f"act_lo{i}") for i in range(2)]
        pro_act_dt = sem("pro_act_dt")
        pro_dve_a = sem("pro_dve_a")
        pv_set = sem("pv_set")
        x_ssq = sem("x_ssq")
        x_sqrt = sem("x_sqrt")
        xr_set = sem("xr_set")
        kp_zero = sem("kp_zero")
        w_phasor = sem("w_phasor")
        b_scaled = sem("b_scaled")
        ta_set = sem("ta_set")
        tb_set = sem("tb_set")
        pw_set = sem("pw_set")
        pr_set = sem("pr_set")
        powers = sem("powers")
        cs_in = sem("cs_in")
        lam_in = sem("lam_in")
        fgain_in = sem("fgain_in")
        lam_sum = sem("lam_sum")
        lam_exp = sem("lam_exp")
        rope_sw = sem("rope_sw")
        qk_set = sem("qk_set")
        v_norm = sem("v_norm")
        v_turned = sem("v_turned")
        v_set = sem("v_set")
        mask_set = sem("mask_set")
        head_in = sem("head_in")
        first = sem("first")
        sc_ps = sem("sc_ps")
        max_set = sem("max_set")
        probs_set = sem("probs_set")
        diff_set = sem("diff_set")
        pt_ps = sem("pt_ps")
        at_set = sem("at_set")
        o_ps = sem("o_ps")
        o_set = sem("o_set")
        o_sq = sem("o_sq")
        sub_root = sem("sub_root")
        on_set = sem("on_set")
        ot_ps = sem("ot_ps")
        o_hi = sem("o_hi")
        o_lo = sem("o_lo")
        yt_ps = sem("yt_ps")
        y_set = sem("y_set")
        y_sqs = sem("y_sqs")
        y_root = sem("y_root")
        y_out = sem("y_out")
        out_done = sem("out_done")

        def power_table(cmul, t1, t2, first, n, t):
            for m in (1, 2, 4, 8):
                if m < n:
                    k = 2 * (first * m).bit_length() - 4
                    c = min(m, n - m)
                    cmul((t1[:, :, m:m + c], t2[:, :, m:m + c]), (t1[:, :, 0:c], t2[:, :, 0:c]),
                         [pw[:, k + i].unsqueeze(2).broadcast_to([P, G, c]) for i in range(2)],
                         [x[:, 0:G * c].rearrange("p (g n) -> p g n", g=G) for x in t])

        def normed_x(V, b, par):
            V.tensor_tensor(xn[:, :], xb[:, par].rearrange("k j (g c) -> k g j c", c=GC),
                            ssq[:, 0].unsqueeze(1).unsqueeze(3).broadcast_to([NK, BG, T, GC]), ALU.mult).then_inc(xn_set, 1)

        def input_powers(V, link, F, b, t):
            over = lambda x: x[:, ds(b * BG, BG)].unsqueeze(2).broadcast_to([P, BG, T, GC])
            at_j = lambda x: (x[:, :, ds(b * BG, BG)].rearrange("p j g -> p g j").unsqueeze(3)
                              .broadcast_to([P, BG, T, GC]))
            t = t.rearrange("p (g j c) -> p g j c", g=BG, j=T)
            V.tensor_tensor(F[:, :], at_j(PR1), over(Bst), ALU.mult)
            link(V.tensor_tensor(t, at_j(PR2), over(Bsw), ALU.mult))
            V.tensor_tensor(F[:, :], F[:, :], t, ALU.add).then_inc(f_set, 1)

        block = ctx.enter_context(nc.Block())

        def ffn_loads(sp, l):
            nu, nd = (U_UP0, U_DN0) if l == 0 else (U_UP1, U_DN1)
            with sp.Fori(0, FT // 2) as i:
                for c in range(4):
                    load_unit(sp, i * 4 + (nu + c), cols(up_w[l], i * (2 * P) + ((c % 2) * FF + (c // 2) * P)), c)
            with sp.Fori(0, 2) as i:
                for c in range(12):
                    kc, nk = c % 3, (8, 8, 6)[c % 3]
                    load_unit(sp, i * 12 + (nd + c),
                              cols(down_w[l], i * (4 * P) + (c // 3) * P, kc * D, nk), c, nk)

        @block.sync
        def _(sp):
            sp.dma_start(cst[:, :], consts[:, 0:514]).then_inc(s_const, 16)
            sp.wait_ge(s_an, 96)
            sp.wait_ge(s_bn, 32)
            sp.wait_ge(s_cn, 32)
            sp.wait_ge(s_dt, 16)
            sp.dma_start(X2[0:2], inp["meta_tokens"].rearrange("(k j) d -> k j d", j=T)).then_inc(s_x2, 16)
            sp.dma_start(X2[2:NK], inp["x"][0].rearrange("(k j) d -> k j d", j=T)).then_inc(s_x2, 16)
            for i in range(2):
                load_unit(sp, i, cols(glu_w[0], (i % 2) * D), i)

            def load_xb(b, par):
                sp.dma_start(xb[0:2, par], inp["meta_tokens"][:, ds(b * P, P)]
                             .rearrange("(k j) d -> k j d", j=T)).then_inc(xb_in[par], 16)
                sp.dma_start(xb[2:NK, par], inp["x"][0][:, ds(b * P, P)]
                             .rearrange("(k j) d -> k j d", j=T)).then_inc(xb_in[par], 16)

            def toeplitz(b, par):
                sp.wait_ge(kp_set, b + 1)
                for i in range(T):
                    sp.dma_start(TT[i * GC:(i + 1) * GC, par],
                                 Kp[:, :, (T - 1 - i) * GC:(T - 1 - i) * GC + P]).then_inc(tt_in[par], 16)

            load_xb(0, 0)
            load_xb(1, 1)
            toeplitz(0, 0)

            def load_next(b, par):
                sp.wait_ge(xt_ps, b - 1)
                sp.wait_ge(xn_set, b - 1)
                load_xb(b, par)

            load_next(2, 0)
            toeplitz(1, 1)
            with sp.Fori(0, 2) as i:
                for par in range(2):
                    load_next(i * 2 + (par + 3), 1 - par)
                    toeplitz(i * 2 + (par + 2), par)
            load_next(7, 1)
            toeplitz(6, 0)
            toeplitz(7, 1)
            for n in range(2, 16):
                load_unit(sp, n, cols(glu_w[0], (n % 2) * D + (n // 2) * P), n)
            ffn_loads(sp, 0)
            sp.dma_start(cs[:, :].rearrange("p a t -> p (a t)"), consts[:, 514:514 + 2 * L]).then_inc(cs_in, 16)
            with sp.Fori(0, 6) as i:
                for c in range(4):
                    load_unit(sp, i * 4 + (U_QKV + c), cols(qkv_w[0], i * (4 * P) + c * P), c)
            with sp.Fori(0, 2) as i:
                for c in range(4):
                    load_unit(sp, i * 4 + (U_WO + c), cols(wo_w[0], i * (4 * P) + c * P), c)
            ffn_loads(sp, 1)
            for t in range(SEQ // P):
                sp.wait_ge(y_out, t + 1)
                sp.dma_start(out[0][t * P:(t + 1) * P, :], ytok[:, t]).then_inc(out_done, 16)
            sp.wait_ge(out_done, 16 * (SEQ // P))

        @block.tensor
        def _(pe):
            for s in (v_turned, ot_ps, yt_ps):
                pe.sem_inc(s, FREE)
            pe.wait_ge(s_const, 16)
            pe.wait_ge(ones_set, 1)
            pe.wait_ge(s_an, 96)
            for i, (src, n) in enumerate(((an[:, 0].rearrange("g a n -> g (a n)"), P),
                                          (an[:, 1].rearrange("g a n -> g (a n)"), P),
                                          (gd[:, 0:T].rearrange("g j c -> g (j c)"), P),
                                          (gd[:, T], GC))):
                mm = nc.tensor.transpose(ps[0:n, 1, i * G:(i + 1) * G], src, ident[0:G, 0:G])
            mm.then_inc(pro_ps, 1)
            pe.wait_ge(s_bn, 32)
            for c in range(GC):
                mm = nc.tensor.transpose(ps[:, 2 + c // 8, (c % 8) * G:(c % 8 + 1) * G],
                                         Bn[:, :, :].rearrange("g a n -> g (a n)")[:, c:2 * D:GC], ident[0:G, 0:G])
            mm.then_inc(pro_ps, 1)
            pe.wait_ge(s_cn, 32)
            for t in range(CT):
                mm = nc.tensor.transpose(ps[:, 4 + t // 4, (t % 4) * P:(t % 4 + 1) * P],
                                         Cn[:, t].rearrange("p a n -> p (a n)"), ident)
            mm.then_inc(pro_ps, 1)
            pe.wait_ge(s_vec, 16 * 8)
            for t, rows in enumerate((P, P, 96, 49)):
                mm = nc.tensor.transpose(ps[:, 0, t * P:t * P + rows], vstage[0:rows, t], ident[0:rows, 0:rows])
            mm.then_inc(pro_ps, 1)
            pe.wait_ge(pro_act, 1)
            for h in range(2):
                mm = nc.tensor.matmul(ps[:, 6 + h, :], swap64, Bst[:, 32 * h:32 * h + 32], start=True, stop=True)
            mm.then_inc(pro_ps, 1)
            pe.wait_ge(pro_act, 2)
            for h in range(2):
                mm = nc.tensor.matmul(ps[:, 2 + h, :], swap64, Q1[:, 32 * h:32 * h + 32], start=True, stop=True)
            mm.then_inc(pro_ps, 1)

            def x_transposes(b, par):
                pe.wait_ge(xb_in[par], b16(b, par))
                if not isinstance(b, int) or b >= 2:
                    pe.wait_ge(z_lo, b - 1)
                elif b == 0:
                    pe.wait_ge(pro_act, 3)
                for j in range(T):
                    mm = nc.tensor.transpose(ps[:, j // 4, (j % 4) * NK:(j % 4 + 1) * NK],
                                             xb[:, par, j], ident[0:NK, 0:NK])
                mm.then_inc(xt_ps, 1)

            def b16(b, par):
                return (b - par) * 16 + 32

            def u_transposes(b, par):
                pe.wait_ge(xn_set, b + 1)
                if not isinstance(b, int) or b >= 1:
                    pe.wait_ge(v_read, b)
                else:
                    pe.wait_ge(pro_act, 3)
                for g in range(BG):
                    mm = nc.tensor.transpose(ps[:, 4 + g // 4, (g % 4) * NK:(g % 4 + 1) * NK],
                                             xn[:, g].rearrange("k j c -> k (j c)"), ident[0:NK, 0:NK])
                mm.then_inc(u_ps, 1)
                pe.wait_ge(f_set, b + 1)
                for g in range(BG):
                    mm = nc.tensor.transpose(ps[:, 2 + g // 4, (g % 4) * P:(g % 4 + 1) * P],
                                             F[:, g].rearrange("p j c -> p (j c)"), ident)
                mm.then_inc(ft_ps, 1)

            def kernel_products(b, par):
                pe.wait_ge(e_set, b + 1)
                pe.wait_ge(u_set, b + 1)
                for g in range(BG):
                    mm = nc.tensor.matmul(ps[0:GC, 4 + g // 4, (g % 4) * P:(g % 4 + 1) * P],
                                          F[:, g, T - 1], E[:, par, g, 0:T], start=True, stop=True)
                mm.then_inc(k_ps, 1)

            def inject(b, par):
                pe.wait_ge(wbt_set, b + 1)
                pe.wait_ge(k_copied, b + 1)
                for g in range(BG):
                    for sw in range(2):
                        for half in range(2):
                            mm = nc.tensor.matmul(
                                ps[64 * half:64 * half + 64, 2 + 2 * sw + g // 4, (g % 4) * NK:(g % 4 + 1) * NK],
                                WBT[:, g, 64 * (half ^ sw):64 * (half ^ sw) + 64], U[:, par, g],
                                start=True, stop=True)
                mm.then_inc(v_ps, 1)

            def swapped_states(b):
                pe.wait_ge(z_scanned, b + 1)
                if not isinstance(b, int) or b >= 1:
                    pe.wait_ge(gelu_set, b)
                for h in range(2):
                    mm = nc.tensor.matmul(ps[:, 6 + h, 0:4 * NK], swap64, zst[:, 4 * h:4 * h + 4],
                                          start=True, stop=True)
                mm.then_inc(zsw_ps, 1)

            def outputs(b, par, done):
                pe.wait_ge(s_set, b + 1)
                pe.wait_ge(tt_in[par], done)
                for g in range(BG):
                    o = ps[0:NK, 6 + g // 4, (g % 4) * P:(g % 4 + 1) * P]
                    nc.tensor.matmul(o, Sst[:, g], E[:, par, g, 1:T + 1], start=True, stop=False)
                    mm = nc.tensor.matmul(o, U[:, par, g], TT[:, par, g], start=False, stop=True)
                mm.then_inc(y_ps, 1)

            def z_transposes(b):
                pe.wait_ge(gelu_set, b + 1)
                for j in range(T):
                    mm = nc.tensor.transpose(ps[:, j // 4, (j % 4) * NK:(j % 4 + 1) * NK],
                                             Z2[:, j], ident[0:NK, 0:NK])
                mm.then_inc(zt_ps, 1)

            x_transposes(0, 0)
            u_transposes(0, 0)
            kernel_products(0, 0)

            def step(b, par, more, first=False):
                inject(b, par)
                if not first:
                    pe.wait_ge(xt_out, b + 1)
                    z_transposes(b - 1)
                if more:
                    u_transposes(b + 1, 1 - par)
                swapped_states(b)
                if more:
                    x_transposes(b + 1, 1 - par)
                    kernel_products(b + 1, 1 - par)
                outputs(b, par, (b - par) * 64 + 128)

            step(0, 0, True, first=True)
            step(1, 1, True)
            with pe.Fori(0, 2) as i:
                for par in range(2):
                    step(i * 2 + (par + 2), par, True)
            step(6, 0, True)
            step(7, 1, False)
            z_transposes(7)

            def stat_products(i):
                pe.wait_ge(sq_sum[i], CT)
                for b in range(2):
                    mm = nc.tensor.matmul(ps[:, STAT[i] + b, 0:264], ones[:, :], acc[:, 264 * b:264 * b + 264],
                                          start=True, stop=True)
                mm.then_inc(stat_ps[i], 1)

            def hg_ready(i):
                def ready(kt):
                    pe.wait_ge(hg_hi[i], kt + 1)
                    pe.wait_ge(hg_lo[i], kt + 1)
                return ready

            def z_ready(kt):
                pe.wait_ge(z_lo, kt + 1)

            def glu():
                with pe.Fori(0, 4) as i:
                    for q in range(2):
                        pe.wait_ge(glu_free, i * 2 + q + FREE)
                        for c in range(2):
                            unit_products(pe, i * 4 + 2 * q + c, 2 * q + c, (4, 0)[q] + 2 * c, actH, actL, ALL,
                                          0, 8, True, True, z_ready if c == 0 and q == 0 else None)

            def ffn(l, spans, spans_down):
                nu, nd = (U_UP0, U_DN0) if l == 0 else (U_UP1, U_DN1)

                def pair(p, q, first=False):
                    if not first:
                        pe.wait_ge(up_free[l], p + FREE)
                    for c in range(2):
                        if first and q and c:
                            pe.wait_ge(stat_sqrt[2 * l], 1)
                        unit_products(pe, p * 2 + (nu + c), 2 * q + c, 4 * (1 - q) + 2 * c, hgH, hgL, spans,
                                      0, 8, True, True, hg_ready(2 * l) if p0(p) and c == 0 else None)

                p0 = lambda p: isinstance(p, int) and p == 0
                if l == 0:
                    pe.wait_ge(glu_free, CT + FREE)
                pair(0, 0, first=True)
                stat_products(2 * l)
                pair(1, 1, first=True)
                with pe.Fori(0, FT // 2 - 1) as i:
                    for q in range(2):
                        pair(i * 2 + (2 + q), q)
                pe.wait_ge(up_free[l], FT + FREE)
                with pe.Fori(0, 2) as i:
                    for m in range(4):
                        pe.wait_ge(h_new[1 + 2 * l], (i * 4 + (m - 1) if m else i * 3) + FREE)
                        for kc in range(3):
                            def ready(kt):
                                pe.wait_ge(act_hi[l], kt + 1)
                                pe.wait_ge(act_lo[l], kt + 1)
                            nk = (8, 8, 6)[kc]
                            unit_products(pe, i * 12 + (nd + 3 * m + kc), (3 * m + kc) % 4, 4 + 2 * (m % 2), actH, actL,
                                          spans_down, 8 * kc, nk, kc == 0, kc == 2, ready if m == 0 else None)
                        if l == 1 and m:
                            y_transposes(i * 4, i * 4 + m, m - 1)
                    if l == 1:
                        y_transposes(i * 4, i * 4 + 4, 3)

            def y_transposes(ct, n, m):
                pe.wait_ge(h_new[3], n + FREE)
                free = n - 2 if m else ct
                pe.wait_ge(y_set, free + FREE)
                pe.wait_ge(y_sqs, free * 4 + FREE)
                for t in range(SEQ // P):
                    mm = nc.tensor.transpose(ps[:, m % 2, t * P:(t + 1) * P],
                                             (cg, cv)[m % 2][:, t * P:(t + 1) * P], ident)
                mm.then_inc(yt_ps, 1)

            def qkv():
                def tile(n, m, ready=None):
                    unit_products(pe, n + U_QKV, m, 2 * m, hgH, hgL, ALL, 0, 8, True, True, ready)

                tile(0, 0, hg_ready(1))
                stat_products(1)
                tile(1, 1)
                tile(2, 2)
                pe.wait_ge(stat_sqrt[1], 1)
                tile(3, 3)
                with pe.Fori(0, 3) as i:
                    for m in range(4):
                        pe.wait_ge(qk_set, i * 4 + (2 + m + FREE))
                        tile(i * 4 + (4 + m), m)

                def v_transposes(n, m):
                    pe.wait_ge(v_norm, n + FREE)
                    if m == 0:
                        pe.wait_ge(qk_set, 2 * HEADS + 1 + FREE)
                    pe.wait_ge(v_set, (n - 2 if m else n - 1) + FREE)
                    for t, (t0, tn) in enumerate(TILES):
                        o = (ps[0:tn, 5 + 2 * (m % 2), 0:P] if t == 0 else
                             ps[:, 4 + 2 * (m % 2), (t - 1) * P:t * P])
                        mm = nc.tensor.transpose(o, (cg, cv)[m % 2][:, t0:t0 + tn], ident)
                    mm.then_inc(v_turned, 1)

                pe.wait_ge(qk_set, 2 * HEADS - 1 + FREE)
                with pe.Fori(0, 2) as i:
                    for m in range(4):
                        n = i * 4 + m
                        pe.wait_ge(v_norm, (n - 1 if m else i * 3) + FREE)
                        unit_products(pe, n + (U_QKV + 2 * HEADS), m, 2 * (m % 2), hgH, hgL, ALL, 0, 8, True, True)
                        if m:
                            v_transposes(n, m - 1)
                    v_transposes(i * 4 + 4, 3)

            def scores(h, i, n):
                q0, nq = TILES[i + 1]
                nk = q0 + nq
                for c in range(2):
                    if not isinstance(n, int) or n:
                        pe.wait_ge(probs_set, n * 2 + (c - 1))
                    if c == 0 and i == 0:
                        pe.wait_ge(head_in, h + 1)
                    half = slice(HD * c, HD * c + HD)
                    pieces = [(0, PS_COL, 0, min(nk, CUT))] + ([(1, -CUT, CUT, nk)] if nk > CUT else [])
                    for bank, col, a, b in pieces:
                        nc.tensor.matmul(ps[:, 2 * c + bank, a + col:b + col], qs[half, q0:nk], ks[half, a:b],
                                         start=True, stop=b < nk)
                    nc.tensor.matmul(ps[:, 2 * c + bank, q0 + col:nk + col], identB[:, :], maskB[:, :],
                                     start=False, stop=True).then_inc(sc_ps, 1)

            def attend(h, n, i, par, first_head=False, last=False):
                pe.wait_ge(diff_set, n + 1)
                for t in (*range(1, i + 2), 0):
                    k0, kn = TILES[t]
                    o = ps[0:kn, 6, 0:P] if t == 0 else ps[:, 4, (t - 1) * P:t * P]
                    mm = nc.tensor.transpose(o, Ab[:, k0:k0 + kn], ident)
                mm.then_inc(pt_ps, 1)
                if not (last and i >= NQ - 2):
                    scores(h + 1 if i >= NQ - 2 else h, (i + 2) % NQ, n + 2)
                if i == 3 and not first_head:
                    turn_head(h - 1)
                pe.wait_ge(o_set, n)
                pe.wait_ge(at_set, n + 1)
                for t in (*range(1, i + 2), 0):
                    kn = TILES[t][1]
                    mm = nc.tensor.matmul(ps[:, 5, P:2 * P], AT[0:kn, t, :], vtok[0:kn, t, ds(h * P, P)],
                                          start=t == 1, stop=t == 0)
                mm.then_inc(o_ps, 1)

            def turn_head(h):
                pe.wait_ge(first, 13)
                pe.wait_ge(on_set, h + 1)
                pe.wait_ge(o_lo, h + FREE)
                for t in range(NQ):
                    mm = nc.tensor.transpose(ps[:, 7, t * P:(t + 1) * P], On[:, t], ident)
                mm.then_inc(ot_ps, 1)

            def first_scores():
                pe.wait_ge(mask_set, 1)
                pe.wait_ge(qk_set, 2 * HEADS + 1 + FREE)
                pe.wait_ge(v_set, HEADS - 1 + FREE)
                for h in range(HEADS):
                    for c in range(2):
                        half = slice(HD * c, HD * c + HD)
                        o = ps[0:META, 4 + c, h * META:(h + 1) * META]
                        nc.tensor.matmul(o, qk[half, h, 0:META], qk[half, HEADS + h, 0:META], start=True, stop=False)
                        mm = nc.tensor.matmul(o, identB[:, 0:META], maskB[:, 0:META], start=False, stop=True)
                mm.then_inc(first, 1)

            def first_turned():
                pe.wait_ge(first, 4)
                for h in range(HEADS):
                    mm = nc.tensor.transpose(ps[0:META, 5, h * META:(h + 1) * META], A0[:, h],
                                             ident[0:META, 0:META])
                mm.then_inc(first, 1)

            def first_output():
                pe.wait_ge(first, 6)
                for h in range(HEADS):
                    mm = nc.tensor.matmul(ps[0:META, 6 + h // 4, (h % 4) * P:(h % 4 + 1) * P], AT0[:, h],
                                          vtok[0:META, 0, h * P:(h + 1) * P], start=True, stop=True)
                mm.then_inc(first, 1)

            def first_back():
                pe.wait_ge(first, 10)
                for h in range(HEADS):
                    mm = nc.tensor.transpose(ps[:, 7, h * META:(h + 1) * META], ON0[:, h], ident[0:META, 0:META])
                mm.then_inc(first, 1)

            def attention():
                first_scores()
                pe.wait_ge(v_norm, HEADS + FREE)
                scores(0, 0, 0)
                scores(0, 1, 1)
                first_turned()
                pe.wait_ge(v_set, HEADS + FREE)
                first_output()
                pe.wait_ge(first, 8)
                for i in range(NQ):
                    attend(0, i, i, 0, first_head=True)
                    if i == 2:
                        first_back()
                with pe.Fori(0, HEADS // 2 - 1) as h:
                    for i in range(2 * NQ):
                        attend(h * 2 + (1 + i // NQ), h * (2 * NQ) + (NQ + i), i % NQ, 1 - i // NQ)
                for i in range(NQ):
                    attend(HEADS - 1, (HEADS - 1) * NQ + i, i, 1, last=True)

            def out_projection():
                def ready(kt):
                    if kt == 0:
                        pe.wait_ge(first, 13)
                    if kt == HEADS - 1:
                        turn_head(HEADS - 1)
                    pe.wait_ge(o_hi, kt + 1)
                    pe.wait_ge(o_lo, kt + 1 + FREE)
                for n in range(CT):
                    if n >= 2:
                        pe.wait_ge(h_new[2], n - 1 + FREE)
                    unit_products(pe, U_WO + n, n % 4, 2 * (n % 2), oH, oL, ALL, 0, 8, True, True,
                                  ready if n == 0 else None)

            glu()
            ffn(0, ALL, ALL)
            qkv()
            attention()
            out_projection()
            ffn(1, FROM12, FROM16)

        @block.scalar
        def _(act):
            for s in (v_set, y_sqs):
                act.sem_inc(s, FREE)
            for c in range(2):
                act.dma_start(an[:, 0, c], inp["s5_a_re"][0]).then_inc(s_an, 16)
                act.dma_start(an[:, 1, c], inp["s5_a_im"][0]).then_inc(s_an, 16)
            act.dma_start(gd[:, 0:T], inp["norm_mix_gain"][0].rearrange("(g c) -> g c", c=GC).unsqueeze(1)
                          .broadcast_to([G, T, GC])).then_inc(s_an, 16)
            act.dma_start(gd[:, T], inp["s5_d"][0].rearrange("(g c) -> g c", c=GC)).then_inc(s_an, 16)
            act.dma_start(sm[:, 0], inp["s5_log_dt"].broadcast_to([P, G])).then_inc(s_dt, 16)
            act.dma_start(Bn[:, 0], inp["s5_b_re"][0].rearrange("g n c -> g (n c)")).then_inc(s_bn, 16)
            act.dma_start(Bn[:, 1], inp["s5_b_im"][0].rearrange("g n c -> g (n c)")).then_inc(s_bn, 16)
            for c, name in enumerate(("s5_c_re", "s5_c_im")):
                act.dma_start(Cn[:, :, c], inp[name][0].rearrange("(t g) c n -> (g c) t n", t=CT)).then_inc(s_cn, 16)
            act.dma_start(lam, inp["attn_lambda"][0].rearrange("a b -> (a b)").unsqueeze(0)
                          .broadcast_to([P, 4 * HD])).then_inc(lam_in, 16)
            cw = inp["ffn_conv_w"].rearrange("l j (t p) -> (l j t) p", p=P)
            rows = lambda a: a.rearrange("l (t p) -> (l t) p", p=P)
            for t, r0, src in ((0, 0, cw[0:P]), (1, 0, cw[P:2 * P]), (2, 0, cw[2 * P:264]),
                               (2, 8, rows(inp["ffn_conv_b"])), (3, 0, rows(inp["norm_mix_gain"])),
                               (3, 16, rows(inp["norm_ffn_gain"])), (3, 32, rows(inp["s5_b_glu"])),
                               (3, 48, inp["attn_subln_gain"])):
                act.dma_start(vstage[r0:r0 + src.shape[0], t], src).then_inc(s_vec, 16)

            act.wait_ge(ones_set, 1)
            act.wait_ge(s_dt, 16)
            nc.scalar.activation(sm[:, 1], sm[:, 0], ACT.Exp).then_inc(pro_act_dt, 1)
            act.wait_ge(pro_ps, 2)
            for h in range(2):
                bps = ps[:, 2 + h, :].rearrange("p (c g) -> p g c", c=8)
                ins = nc.scalar.activation(Bst[:, :, 8 * h:8 * h + 8], bps, ACT.Copy)
            ins.then_inc(pro_act, 1)
            act.wait_ge(pro_ps, 3)
            for h in range(2):
                ins = nc.scalar.activation(Q1[:, 32 * h:32 * h + 32], ps[:, 4 + h, :], ACT.Copy, scale=sgn)
            ins.then_inc(pro_act, 1)
            act.wait_ge(pro_dve_a, 1)
            nc.scalar.activation(sm[:, 2], sm[:, 9], ACT.Exp)
            nc.scalar.activation(rho[:, :], sm[:, 9], ACT.Exp, scale=8.0)
            act.wait_ge(pro_dve_a, 2)
            nc.scalar.activation(sm[:, 4], sm[:, 10], ACT.Sin)
            nc.scalar.activation(sm[:, 5], sm[:, 6], ACT.Sin).then_inc(pro_act_dt, 1)
            act.wait_ge(pro_ps, 4)
            nc.scalar.activation(PV[:, 0:352], ps[:, 0, 0:352], ACT.Copy)
            nc.scalar.activation(PV[:, 352:401], ps[:, 0, 384:433], ACT.Copy).then_inc(pv_set, 1)
            act.wait_ge(pro_ps, 5)
            for h in range(2):
                ins = nc.scalar.activation(Bsw[:, 32 * h:32 * h + 32], ps[:, 6 + h, :], ACT.Copy)
            act.wait_ge(pro_ps, 6)
            for h in range(2):
                ins = nc.scalar.activation(Q2[:, 32 * h:32 * h + 32], ps[:, 2 + h, :], ACT.Copy, scale=-1.0)
            ins.then_inc(pro_act, 1)
            act.wait_ge(powers, 1)
            for j in range(T):
                nc.scalar.activation(PR1[:, j], P1[:, T - 1 - j], ACT.Copy)
                ins = nc.scalar.activation(PR2[:, j], P2[:, T - 1 - j], ACT.Copy)
            ins.then_inc(pr_set, 1)
            act.wait_ge(s_x2, 32)
            for j in range(T):
                nc.scalar.activation(junk[0:NK], X2[:, j], ACT.Square,
                                     accum_out=ssq[:, 0, j:j + 1]).then_inc(act_seq, 1)
                act.wait_ge(act_seq, j + 1)
            act.wait_ge(x_ssq, 1)
            nc.scalar.activation(ssq[:, 2], ssq[:, 1], ACT.Sqrt).then_inc(x_sqrt, 1)
            for n in range(2):
                split_hi(act, n, n, 0)

            def turn_out(b, par):
                act.wait_ge(xt_ps, b + 1)
                for h in range(2):
                    o = hT[:, ds(b, 1)].rearrange("p a (k j) -> p (a j) k", j=T)[:, 4 * h:4 * h + 4]
                    ins = nc.scalar.activation(o, ps[:, h, 0:4 * NK].rearrange("p (j k) -> p j k", j=4), ACT.Copy)
                ins.then_inc(xt_out, 1)

            def input_weights(b, par):
                act.wait_ge(ft_ps, b + 1)
                if not isinstance(b, int) or b >= 1:
                    act.wait_ge(v_ps, b)
                for h in range(2):
                    ins = nc.scalar.activation(WBT[:, 4 * h:4 * h + 4], ps[:, 2 + h, :], ACT.Copy)
                ins.then_inc(wbt_set, 1)

            def kernel_out(b, par):
                act.wait_ge(k_ps, b + 1)
                if not isinstance(b, int) or b >= 1:
                    act.wait_ge(tt_in[1 - par], tt_done(b - 1, 1 - par))
                else:
                    act.wait_ge(kp_zero, 1)
                for h in range(2):
                    ins = nc.scalar.activation(
                        Kp[:, 4 * h:4 * h + 4, 7 * GC:15 * GC],
                        ps[0:GC, 4 + h, :].rearrange("p (g c) -> p g c", g=4), ACT.Copy)
                ins.then_inc(k_copied, 1)

            def tt_done(b, par):
                return (b - par) * 64 + 128

            def gelu(b):
                act.wait_ge(y_ps, b + 1)
                if not isinstance(b, int) or b >= 1:
                    act.wait_ge(zt_ps, b)
                for h in range(2):
                    o = Z2[:, :, 64 * h:64 * h + 64].rearrange("k j (g c) -> k g j c", g=4)
                    ins = nc.scalar.activation(
                        o, ps[0:NK, 6 + h, :].rearrange("k (g j c) -> k g j c", g=4, j=T), ACT.Gelu_apprx_tanh)
                ins.then_inc(gelu_set, 1)

            def z_round(b):
                act.wait_ge(zt_ps, b + 1)
                for h in range(2):
                    o = actH[:, ds(b, 1)].rearrange("p a (k j) -> p (a j) k", j=T)[:, 4 * h:4 * h + 4]
                    ins = nc.scalar.activation(o, ps[:, h, 0:4 * NK].rearrange("p (j k) -> p j k", j=4), ACT.Copy)
                ins.then_inc(z_hi, 1)

            turn_out(0, 0)
            input_weights(0, 0)
            kernel_out(0, 0)

            def step(b, par, more, first=False):
                if not first:
                    z_round(b - 1)
                if more:
                    input_weights(b + 1, 1 - par)
                    turn_out(b + 1, 1 - par)
                    kernel_out(b + 1, 1 - par)
                gelu(b)

            step(0, 0, True, first=True)
            step(1, 1, True)
            with act.Fori(0, 2) as i:
                for par in range(2):
                    step(i * 2 + (par + 2), par, True)
            step(6, 0, True)
            step(7, 1, False)
            z_round(7)

            def round_hg(i, ct, gain, new):
                act.wait_ge(h_new[new[0]], new[1] + FREE)
                nc.scalar.activation(hgH[:, ds(ct, 1)], hT[:, ds(ct, 1)], ACT.Copy,
                                     scale=PV[:, ds(gain, 1)]).then_inc(hg_hi[i], 1)

            def glu():
                act.wait_ge(z_lo, CT)
                for n in (2, 3):
                    split_hi(act, n, n, 1)
                with act.Fori(0, 4) as i:
                    for q in range(2):
                        n = i * 4 + 2 * q
                        for c in range(2):
                            split_hi(act, n + (4 + c), 2 * q + c, i * 2 + (2 + q))
                        act.wait_ge(w_used, n + 2)
                        gate = ps[:, (6, 2)[q]:(6, 2)[q] + 2, 0:264]
                        nc.scalar.activation(span(cg, ALL), gate, ACT.Sigmoid,
                                             bias=PV[:, ds(i * 2 + (B_GLU + 8 + q), 1)]).then_inc(glu_sig, 1)
                        round_hg(0, i * 2 + q, i * 2 + (GAIN_FFN + q), (0, i * 2 + (q + 1)))

            def root(i):
                act.wait_ge(stat_ps[i], 1)
                nc.scalar.activation(span(sqt, ALL), ps[:, STAT[i]:STAT[i] + 2, 0:264], ACT.Sqrt, bias=eps_col,
                                     scale=1.0 / D).then_inc(stat_sqrt[i], 1)

            def ffn(l, spans, t0):
                nu, nd = (U_UP0, U_DN0) if l == 0 else (U_UP1, U_DN1)
                root(2 * l)
                with act.Fori(0, FT // 2) as i:
                    for q in range(2):
                        for c in range(2):
                            split_hi(act, i * 4 + (nu + 4 + 2 * q + c), 2 * q + c, i * 2 + (nu // 2 + 2 + q))
                        act.wait_ge(conv_gate[l], i * 2 + (q + 1))
                        nc.scalar.activation(cg[:, t0:], cg[:, t0:], ACT.Silu).then_inc(silu_set[l], 1)
                        act.wait_ge(act_set[l], i * 2 + (q + 1))
                        nc.scalar.activation(actH[:, ds(i * 2 + q, 1), t0:], cg[:, t0:].unsqueeze(1),
                                             ACT.Copy).then_inc(act_hi[l], 1)
                if l == 0:
                    with act.Fori(0, 2) as i:
                        for m in range(4):
                            for c in range(3 * m, 3 * m + 3):
                                split_hi(act, i * 12 + (nd + 4 + c), c % 4, i * 6 + (nd // 2 + 2 + c // 2),
                                         (8, 8, 6)[(c + 4) % 3] if c < 8 else 8)
                            round_hg(1, i * 4 + m, i * 4 + (GAIN_MIX + 8 + m), (1, i * 4 + (m + 1)))
                else:
                    act.wait_ge(w_used, nd)
                    for c in range(20):
                        split_hi(act, nd + 4 + c, c % 4, (nd + 4 + c) // 2, (8, 8, 6)[(c + 4) % 3])
                        if c % 3 == 2:
                            out_squares(c // 3)
                    for n in (6, 7):
                        out_squares(n)
                    act.wait_ge(y_set, CT + 1 + FREE)
                    nc.scalar.activation(yrt, ytot, ACT.Sqrt, bias=eps_col, scale=1.0 / D).then_inc(y_root, 1)

            def out_squares(n):
                act.wait_ge(y_set, n + 1 + FREE)
                for t in range(SEQ // P):
                    if n + t:
                        act.wait_ge(y_sqs, 4 * n + t + FREE)
                    ins = nc.scalar.activation(ysq[:, :], ps[:, n % 2, t * P:(t + 1) * P], ACT.Square,
                                               accum_out=ysum[:, 4 * n + t:4 * n + t + 1])
                    ins.then_inc(y_sqs, 1)

            def qkv():
                root(1)
                act.wait_ge(w_used, U_QKV)
                nc.scalar.activation(identB[:, :], ident, ACT.Copy)
                nc.scalar.activation(maskB[:, :], mask, ACT.Copy).then_inc(mask_set, 1)
                with act.Fori(0, 4) as i:
                    for m in range(4):
                        split_hi(act, i * 4 + (U_QKV + 4 + m), m, i * 2 + (U_QKV // 2 + 2 + m // 2))
                        act.wait_ge(w_used, i * 4 + (U_QKV + 1 + m))
                        act.wait_ge(qk_set, i * 4 + (m + 1) + FREE)
                        for q in range(4):
                            r = q ^ 1
                            ins = nc.scalar.activation(span(cg[32 * q:32 * q + 32], ALL),
                                                       ps[32 * r:32 * r + 32, 2 * m:2 * m + 2, 0:264], ACT.Copy)
                        ins.then_inc(rope_sw, 1)
                with act.Fori(0, 2) as i:
                    for m in range(4):
                        split_hi(act, i * 4 + (U_QKV + 20 + m), m, i * 2 + (U_QKV // 2 + 10 + m // 2))
                        act.wait_ge(v_turned, i * 4 + (m + 1) + FREE)
                        b = 4 + 2 * (m % 2)
                        o = ds((i * 4 + m) * P, P)
                        nc.scalar.activation(vtok[:, 1:NT, o], ps[:, b].rearrange("p (t c) -> p t c", c=P), ACT.Copy)
                        nc.scalar.activation(vtok[0:META, 0:1, o], ps[0:META, b + 1:b + 2, 0:P],
                                             ACT.Copy).then_inc(v_set, 1)

            def exponentials(n, i):
                nk = sum(TILES[i + 1])
                for c in range(2):
                    act.wait_ge(max_set, n * 2 + (c + 1))
                    nc.scalar.activation(Pb[:, c, 0:nk], score_row(c, P, nk), ACT.Exp, bias=nm[:, c:c + 1],
                                         scale=SCALE, accum_out=esum[:, c:c + 1]).then_inc(probs_set, 1)

            def attend(h, n, i, par, first_head=False, last=False):
                if not (last and i >= NQ - 2):
                    exponentials(n + 2, (i + 2) % NQ)
                if i == 1 and not first_head:
                    head_root(h - 1, 1 - par)
                if i == 3 and not first_head:
                    head_out(h - 1)
                act.wait_ge(o_set, n + 1)
                act.wait_ge(o_sq, n)
                nc.scalar.activation(osq[:, :], Ob[:, par, i], ACT.Square,
                                     accum_out=hsq[par][:, i:i + 1]).then_inc(o_sq, 1)

            def head_root(h, par):
                act.wait_ge(o_sq, (h + 1) * NQ)
                nc.scalar.activation(hrt, hsq[par], ACT.Sqrt, bias=eps_col, scale=1.0 / P).then_inc(sub_root, 1)

            def head_out(h):
                act.wait_ge(ot_ps, h + 1 + FREE)
                nc.scalar.activation(oH[:, ds(h, 1), META:L], turned_row, ACT.Copy, scale=sub_gain).then_inc(o_hi, 1)

            def attention():
                act.dma_start(fgain[:, :], inp["final_norm_gain"].unsqueeze(0).broadcast_to([P, D])).then_inc(fgain_in, 16)
                act.wait_ge(w_used, U_WO)
                act.wait_ge(first, 2)
                nc.scalar.activation(P0[:, :], S0[:, :], ACT.Exp, scale=SCALE).then_inc(first, 1)
                exponentials(0, 0)
                exponentials(1, 1)
                act.wait_ge(first, 8)
                nc.scalar.activation(rt0, sq0, ACT.Sqrt, bias=eps_col[0:META], scale=1.0 / P).then_inc(first, 1)
                for i in range(NQ):
                    attend(0, i, i, 0, first_head=True)
                    if i == 2:
                        act.wait_ge(first, 11)
                        nc.scalar.activation(oH[:, :, 0:META], first_row, ACT.Copy, scale=sub_gain).then_inc(first, 1)
                with act.Fori(0, HEADS // 2 - 1) as h:
                    for i in range(2 * NQ):
                        attend(h * 2 + (1 + i // NQ), h * (2 * NQ) + (NQ + i), i % NQ, 1 - i // NQ)
                for i in range(NQ):
                    attend(HEADS - 1, (HEADS - 1) * NQ + i, i, 1, last=True)
                head_root(HEADS - 1, 1)
                head_out(HEADS - 1)

            def out_projection():
                with act.Fori(0, 2) as i:
                    for m in range(4):
                        split_hi(act, i * 4 + (U_WO + 4 + m), m, i * 2 + (U_WO // 2 + 2 + m // 2))
                        round_hg(2, i * 4 + m, i * 4 + (GAIN_FFN + 8 + m), (2, i * 4 + (m + 1)))

            glu()
            ffn(0, ALL, 0)
            act.wait_ge(lam_sum, 1)
            nc.scalar.activation(lam_e, lam_s, ACT.Exp).then_inc(lam_exp, 1)
            qkv()
            attention()
            out_projection()
            ffn(1, FROM12, META)

        @block.vector
        def _(dve):
            V = nc.vector
            link = Chain(dve, dve_seq)

            def cmul(e, lk, o, a, b, t):
                e.tensor_tensor(t[0], a[0], b[0], ALU.mult)
                e.tensor_tensor(t[1], a[1], b[1], ALU.mult)
                e.tensor_tensor(t[2], a[1], b[0], ALU.mult)
                lk(e.tensor_tensor(t[3], a[0], b[1], ALU.mult))
                e.tensor_tensor(o[0], t[0], t[1], ALU.subtract)
                lk(e.tensor_tensor(o[1], t[2], t[3], ALU.add))

            for s in (glu_free, *up_free, *h_new, qk_set, v_norm, o_lo, y_set):
                dve.sem_inc(s, FREE)
            V.memset(ones[:, :], 1.0)
            V.memset(eps_col, EPS)
            V.memset(P1[:, 0], 1.0)
            V.memset(P2[:, 0], 0.0).then_inc(ones_set, 1)
            dve.wait_ge(pro_ps, 1)
            V.tensor_copy(sm[:, 7:9], ps[:, 1, 0:2 * G].rearrange("p (a g) -> p a g", a=2))
            V.tensor_copy(gainJ[:, :], ps[:, 1, 2 * G:3 * G])
            link(V.tensor_copy(dT[:, :], ps[0:GC, 1, 3 * G:4 * G]))
            dve.wait_ge(s_const, 16)
            dve.wait_ge(pro_act_dt, 1)
            V.tensor_tensor(sm[:, 9], sm[:, 7], sm[:, 1], ALU.mult).then_inc(pro_dve_a, 1)
            link(V.tensor_tensor(sm[:, 11], sm[:, 8], sm[:, 1], ALU.mult))
            link(V.tensor_scalar(sm[:, 12], sm[:, 11], 1.0 / TWO_PI, MAGIC, ALU.mult, ALU.add))
            link(V.tensor_scalar(sm[:, 13], sm[:, 12], MAGIC, None, ALU.subtract))
            link(V.scalar_tensor_tensor(sm[:, 14], sm[:, 13], -PI_A, sm[:, 11], ALU.mult, ALU.add))
            link(V.scalar_tensor_tensor(sm[:, 15], sm[:, 13], -PI_B, sm[:, 14], ALU.mult, ALU.add))
            link(V.scalar_tensor_tensor(sm[:, 14], sm[:, 13], -PI_C, sm[:, 15], ALU.mult, ALU.add))
            link(V.tensor_scalar(sm[:, 10], sm[:, 14], PI_MAX, -PI_MAX, ALU.min, ALU.max))
            link(V.scalar_tensor_tensor(sm[:, 15], sm[:, 10], -1.0, sm[:, 10], ALU.mult, ALU.max))
            V.tensor_scalar(sm[:, 6], sm[:, 15], -1.0, math.pi / 2, ALU.mult, ALU.add).then_inc(pro_dve_a, 1)
            dve.wait_ge(pro_act_dt, 2)
            V.tensor_scalar(sm[:, 6], sm[:, 4], nsgn, None, ALU.mult).then_inc(w_phasor, 1)
            V.tensor_tensor(P1[:, 1], sm[:, 2], sm[:, 5], ALU.mult)
            V.tensor_tensor(sm[:, 17], sm[:, 2], sm[:, 4], ALU.mult)
            link(V.scalar_tensor_tensor(P2[:, 1], sm[:, 4], nsgn, sm[:, 2], ALU.mult, ALU.mult))
            ts = [tmpE[:, k * 4 * G:(k + 1) * 4 * G] for k in range(4)]
            for a, b, o, n in ((1, 1, 2, 1), (1, 2, 3, 2), (1, 4, 5, 4)):
                bc = lambda t: t[:, b:b + 1].broadcast_to([P, n, G])
                cmul(V, link, (P1[:, o:o + n], P2[:, o:o + n]), (P1[:, a:a + n], P2[:, a:a + n]),
                     (bc(P1), bc(P2)), [x[:, 0:n * G].rearrange("p (n g) -> p n g", n=n) for x in ts])
            lr, li, are, aim = sm[:, 7], sm[:, 8], P1[:, 1], sm[:, 17]
            V.tensor_tensor(sm[:, 18], lr, lr, ALU.mult)
            V.tensor_tensor(sm[:, 19], li, li, ALU.mult)
            V.tensor_scalar(sm[:, 20], are, 1.0, None, ALU.subtract).then_inc(powers, 1)
            dve.wait_ge(powers, 1)
            V.tensor_tensor(sm[:, 21], sm[:, 18], sm[:, 19], ALU.add)
            V.tensor_tensor(sm[:, 22], sm[:, 20], lr, ALU.mult)
            V.tensor_tensor(sm[:, 23], aim, li, ALU.mult)
            V.tensor_tensor(sm[:, 24], aim, lr, ALU.mult)
            link(V.tensor_tensor(sm[:, 25], sm[:, 20], li, ALU.mult))
            V.reciprocal(sm[:, 26], sm[:, 21])
            V.tensor_tensor(sm[:, 27], sm[:, 22], sm[:, 23], ALU.add)
            link(V.tensor_tensor(sm[:, 28], sm[:, 24], sm[:, 25], ALU.subtract))
            V.tensor_tensor(sm[:, 29], sm[:, 27], sm[:, 26], ALU.mult)
            link(V.scalar_tensor_tensor(sm[:, 30], sm[:, 28], nsgn, sm[:, 26], ALU.mult, ALU.mult))
            dve.wait_ge(pro_act, 3)
            fre, fim = (sm[:, k].unsqueeze(2).broadcast_to([P, G, GC]) for k in (29, 30))
            sc = [scr[:, k].rearrange("p (g c) -> p g c", g=G) for k in range(4)]
            V.tensor_tensor(sc[0], Bst[:, :, :], fre, ALU.mult)
            V.tensor_tensor(sc[1], Bsw[:, :, :], fim, ALU.mult)
            V.tensor_tensor(sc[2], Bsw[:, :, :], fre, ALU.mult)
            link(V.tensor_tensor(sc[3], Bst[:, :, :], fim, ALU.mult))
            V.tensor_tensor(Bst[:, :, :], sc[0], sc[1], ALU.add)
            V.tensor_tensor(Bsw[:, :, :], sc[2], sc[3], ALU.subtract).then_inc(b_scaled, 1)
            dve.wait_ge(b_scaled, 1)
            dve.wait_ge(pr_set, 1)
            input_powers(V, link, F, 0, tmpE[:, 0:1024])
            dve.wait_ge(f_set, 1)
            dve.wait_ge(act_seq, T)
            V.tensor_scalar(ssq[:, 1], ssq[:, 0], 1.0 / D, EPS, ALU.mult, ALU.add).then_inc(x_ssq, 1)
            V.memset(Kp[:, :, :], 0.0).then_inc(kp_zero, 1)
            V.memset(zin[:, :, 0:1], 0.0)
            V.memset(R[:, :, 0:1], 0.0)
            dve.wait_ge(x_sqrt, 1)
            V.reciprocal(ssq[:, 0], ssq[:, 2]).then_inc(xr_set, 1)
            dve.wait_ge(xr_set, 1)
            dve.wait_ge(xb_in[0], 32)
            normed_x(V, 0, 0)

            def u_out(b, par):
                dve.wait_ge(u_ps, b + 1)
                if not isinstance(b, int) or b >= 2:
                    dve.wait_ge(y_ps, b - 1)
                V.tensor_tensor(U[:, par].rearrange("p (a g) k -> p a g k", a=2),
                                ps[:, 4:6, 0:4 * NK].rearrange("p a (g k) -> p a g k", g=4),
                                gainJ[:, ds(b * BG, BG)].rearrange("p (a g) -> p a g", a=2).unsqueeze(3)
                                .broadcast_to([P, 2, 4, NK]), ALU.mult).then_inc(u_set, 1)

            def tau_c(t, b, n):
                return (t[:, 0:n, ds(b * BG, BG)].rearrange("p t g -> p g t").unsqueeze(3)
                        .broadcast_to([P, BG, n, GC]))

            def over_tau(q, b, n):
                return q[:, ds(b * BG, BG)].unsqueeze(2).broadcast_to([P, BG, n, GC])

            def output_powers(b, par):
                if not isinstance(b, int) or b >= 2:
                    dve.wait_ge(y_ps, b - 1)
                n = T + 1
                e = E[:, par]
                t = tmpE[:, :].rearrange("p (g t c) -> p g t c", g=BG, t=n)
                V.tensor_tensor(e, tau_c(P1, b, n), over_tau(Q1, b, n), ALU.mult)
                link(V.tensor_tensor(t, tau_c(P2, b, n), over_tau(Q2, b, n), ALU.mult))
                ins = V.tensor_tensor(e, e, t, ALU.add)
                ins.then_inc(e_set, 1)
                dve.wait_ge(e_set, b + 1)

            def rotation(b, par):
                ins = V.tensor_copy(R[:, :, 1:NK], rho[:, ds(b * BG, BG)].unsqueeze(2).broadcast_to([P, BG, NK - 1]))
                if isinstance(b, int) and b == 0:
                    ins.then_inc(tb_set, 1)
                dve.wait_ge(ta_set, 1)
                o = T2[:, par].rearrange("p g (a b) -> p g a b", b=8)
                t = tmpE[:, 0:576].rearrange("p (g a b) -> p g a b", g=BG, b=8)
                low = lambda x: x[:, ds(b * BG, BG)].unsqueeze(2).broadcast_to([P, BG, 9, 8])
                high = lambda x: x[:, ds(b * BG, BG)].unsqueeze(3).broadcast_to([P, BG, 9, 8])
                V.tensor_tensor(o, low(TA2), high(TB1), ALU.mult)
                link(V.tensor_tensor(t, low(TA1), high(TB2), ALU.mult))
                link(V.tensor_tensor(o, o, t, ALU.add))

            def kernel_diagonal(b):
                dve.wait_ge(k_copied, b + 1)
                k0 = Kp[:, :, 7 * GC:8 * GC]
                d = tmpE[0:GC, 0:P].rearrange("p (g c) -> p g c", g=BG)
                link(V.tensor_tensor(d, ident[0:GC, 0:GC].unsqueeze(1).broadcast_to([GC, BG, GC]),
                                     dT[:, ds(b * BG, BG)].unsqueeze(2).broadcast_to([GC, BG, GC]), ALU.mult))
                V.tensor_tensor(k0, k0, d, ALU.add).then_inc(kp_set, 1)
                dve.wait_ge(kp_set, b + 1)

            def banks(k, w):
                return ps[:, k:k + 2, 0:4 * NK].rearrange("p a (g k) -> p a g k", g=4)[:, :, :, 0:w]

            def by4(t):
                return t.rearrange("p (a g) k -> p a g k", a=2)

            def scan(b, par):
                dve.wait_ge(v_ps, b + 1)
                dve.wait_ge(t1_set, b + 1)
                w = NK - 1
                V.tensor_tensor(by4(rt1[:, :, 0:w]), by4(T1[:, par, :, 1:NK]), banks(2, w), ALU.mult)
                V.tensor_tensor(by4(rt2[:, :, 0:w]), by4(T2[:, par, :, 1:NK]), banks(4, w), ALU.mult).then_inc(v_read, 1)
                dve.wait_ge(v_read, b + 1)
                link(V.tensor_tensor(zin[:, :, 1:NK], rt1[:, :, 0:w], rt2[:, :, 0:w], ALU.subtract))
                flat = lambda t: t.rearrange("p g k -> p (g k)")
                V.tensor_tensor_scan(flat(zst[:, :, :]), flat(R[:, :, :]), flat(zin[:, :, :]), 0.0,
                                     ALU.mult, ALU.add).then_inc(z_scanned, 1)
                dve.wait_ge(z_scanned, b + 1)

            def states(b, par):
                dve.wait_ge(zsw_ps, b + 1)
                if not isinstance(b, int) or b >= 1:
                    dve.wait_ge(y_ps, b)
                V.tensor_tensor(rt1[:, :, :], T1[:, par, :, 0:NK], zst[:, :, :], ALU.mult)
                link(V.tensor_tensor(by4(rt2[:, :, :]), by4(T2[:, par, :, 0:NK]), banks(6, NK), ALU.mult))
                V.tensor_tensor(Sst[:, :, :], rt1[:, :, :], rt2[:, :, :], ALU.add).then_inc(s_set, 1)
                dve.wait_ge(s_set, b + 1)

            def z_rest(b):
                dve.wait_ge(z_hi, b + 1)
                for h in range(2):
                    v = lambda t: t[:, ds(b, 1)].rearrange("p a (k j) -> p (a j) k", j=T)[:, 4 * h:4 * h + 4]
                    ins = V.tensor_tensor(v(actL), ps[:, h, 0:4 * NK].rearrange("p (j k) -> p j k", j=4),
                                          v(actH).bitcast(F32), ALU.subtract)
                ins.then_inc(z_lo, 1)

            output_powers(0, 0)
            u_out(0, 0)
            dve.wait_ge(pw_set, 1)
            V.memset(TB1[:, :, 0:1], 1.0)
            link(V.memset(TB2[:, :, 0:1], 0.0))
            power_table(lambda *a: cmul(V, link, *a), TB1, TB2, 64, 9, [tmpE[:, k * 256:(k + 1) * 256] for k in range(4)])
            rotation(0, 0)
            kernel_diagonal(0)

            def step(b, par, more, first=False):
                if more:
                    output_powers(b + 1, 1 - par)
                scan(b, par)
                if more:
                    u_out(b + 1, 1 - par)
                if not first:
                    z_rest(b - 1)
                states(b, par)
                if more:
                    kernel_diagonal(b + 1)
                    rotation(b + 1, 1 - par)

            step(0, 0, True, first=True)
            step(1, 1, True)
            with dve.Fori(0, 2) as i:
                link.enter(i, 12)
                for par in range(2):
                    step(i * 2 + (par + 2), par, True)
            link.leave(2)
            step(6, 0, True)
            step(7, 1, False)
            z_rest(7)

            def split_gain(i, ct, gain, n):
                dve.wait_ge(hg_hi[i], n)
                V.scalar_tensor_tensor(hgL[:, ds(ct, 1)], hT[:, ds(ct, 1)], PV[:, ds(gain, 1)],
                                       hgH[:, ds(ct, 1)].bitcast(F32), ALU.mult, ALU.subtract).then_inc(hg_lo[i], 1)

            def glu():
                dve.wait_ge(pv_set, 1)
                V.memset(acc[:, :], 0.0).then_inc(glu_free, 1)
                with dve.Fori(0, 4) as i:
                    for q in range(2):
                        p = i * 2 + q
                        dve.wait_ge(glu_sig, p + 1)
                        V.scalar_tensor_tensor(span(cv, ALL), ps[:, (4, 0)[q]:(4, 0)[q] + 2, 0:264],
                                               PV[:, ds(i * 2 + (B_GLU + q), 1)], span(cg, ALL),
                                               ALU.add, ALU.mult).then_inc(glu_free, 1)
                        dve.wait_ge(glu_free, p + 2 + FREE)
                        V.tensor_tensor(hT[:, ds(p, 1)], hT[:, ds(p, 1)], cv[:, :].unsqueeze(1),
                                        ALU.add).then_inc(h_new[0], 1)
                        split_gain(0, p, i * 2 + (GAIN_FFN + q), p + 1)

            def ffn(l, spans, spans_down, t0):
                nu, nd = (U_UP0, U_DN0) if l == 0 else (U_UP1, U_DN1)
                if l == 0:
                    V.memset(u[:, :, 0:2], 0.0)
                dve.wait_ge(stat_sqrt[2 * l], 1)
                V.reciprocal(rstd[:, :], sqt[:, :]).then_inc(up_free[l], 1)
                dve.wait_ge(up_free[l], 1 + FREE)
                uin = [span(u[:, c, 2:2 + L], spans) for c in range(2)]
                c = (cg, cv)
                col = lambda i, k: PV[:, ds(i * 2 + k, 1)]
                with dve.Fori(0, FT // 2) as i:
                    link.enter(i, 6)
                    for q in range(2):
                        dve.wait_ge(w_used, i * 4 + (nu + 2 * q + 2))
                        V.tensor_tensor(uin[0], pspan(2 * (1 - q), spans), span(rstd, spans), ALU.mult)
                        V.tensor_tensor(uin[1], pspan(2 * (1 - q) + 1, spans), span(rstd, spans),
                                        ALU.mult).then_inc(up_free[l], 1)
                        dve.wait_ge(up_free[l], i * 2 + (q + 2) + FREE)
                        for k in range(2):
                            ins = V.tensor_scalar(c[k][:, t0:], u[:, k, 2 + t0:2 + L],
                                                  col(i, CONV_W + (3 * l + 2) * 2 * FT + k * FT + q),
                                                  col(i, CONV_B + l * 2 * FT + k * FT + q), ALU.mult, ALU.add)
                        link(ins)
                        for j in (1, 0):
                            for k in range(2):
                                ins = V.scalar_tensor_tensor(c[k][:, t0:], u[:, k, t0 + j:L + j],
                                                             col(i, CONV_W + (3 * l + j) * 2 * FT + k * FT + q),
                                                             c[k][:, t0:], ALU.mult, ALU.add)
                                if j == 0 and k == 0:
                                    ins.then_inc(conv_gate[l], 1)
                            link(ins)
                        dve.wait_ge(silu_set[l], i * 2 + (q + 1))
                        V.tensor_tensor(cg[:, t0:], cg[:, t0:], cv[:, t0:], ALU.mult).then_inc(act_set[l], 1)
                        dve.wait_ge(act_hi[l], i * 2 + (q + 1))
                        V.tensor_tensor(actL[:, ds(i * 2 + q, 1), t0:], cg[:, t0:].unsqueeze(1),
                                        actH[:, ds(i * 2 + q, 1), t0:].bitcast(F32), ALU.subtract).then_inc(act_lo[l], 1)
                link.leave(FT // 2)
                if l == 0:
                    with dve.Fori(0, 2) as i:
                        for m in range(4):
                            add_down(l, i * 4 + m, i * 12 + (nd + 3 * m + 3), m, spans_down)
                            split_gain(1, i * 4 + m, i * 4 + (GAIN_MIX + 8 + m), i * 4 + (m + 1))

                else:
                    with dve.Fori(0, 2) as i:
                        link.enter(i, 0)
                        for m in range(4):
                            n = i * 4 + m
                            dve.wait_ge(w_used, i * 12 + (nd + 3 * m + 3))
                            if m >= 2:
                                dve.wait_ge(yt_ps, n - 1 + FREE)
                            else:
                                dve.wait_ge(yt_ps, i * 4 + FREE)
                            h = span(hT[:, ds(n, 1)].rearrange("p a t -> p (a t)"), spans_down)
                            V.tensor_tensor((cg, cv)[m % 2][:, 0:SEQ].rearrange("p (a b) -> p a b", a=2), h,
                                            pspan(2 + m % 2, spans_down), ALU.add).then_inc(h_new[3], 1)
                            if m:
                                y_turned(i * 4 + (m - 1), m - 1)
                        y_turned(i * 4 + 3, 3)
                    link.leave(2)
                    dve.wait_ge(y_sqs, 4 * CT + FREE)
                    V.tensor_reduce(ytot, ysum.rearrange("p (n t) -> p t n", t=4), AX.X, ALU.add).then_inc(y_set, 1)
                    dve.wait_ge(y_root, 1)
                    link(V.reciprocal(yinv, yrt))
                    dve.wait_ge(y_set, CT + 1 + FREE)
                    for t in range(SEQ // P):
                        V.tensor_scalar(ytok[:, t], ytok[:, t], yinv[:, t:t + 1], None, ALU.mult).then_inc(y_out, 1)

            def y_turned(n, m):
                if m == 0:
                    dve.wait_ge(fgain_in, 16)
                dve.wait_ge(yt_ps, n + 1 + FREE)
                V.tensor_tensor(ytok[:, :, ds(n * P, P)], ps[:, m % 2].rearrange("p (t c) -> p t c", c=P),
                                fgain[:, ds(n * P, P)].unsqueeze(1).broadcast_to([P, SEQ // P, P]),
                                ALU.mult).then_inc(y_set, 1)

            def qkv():
                dve.wait_ge(stat_sqrt[1], 1)
                dve.wait_ge(cs_in, 16)
                link(V.reciprocal(rstd[:, :], sqt[:, :]))
                V.tensor_tensor(cs[:, :], cs[:, :], rstd[:, :].unsqueeze(1).broadcast_to([P, 2, L]),
                                ALU.mult).then_inc(qk_set, 1)
                dve.wait_ge(qk_set, 1 + FREE)
                with dve.Fori(0, 4) as i:
                    link.enter(i, 4)
                    for m in range(4):
                        dve.wait_ge(rope_sw, i * 4 + (m + 1))
                        V.tensor_tensor(span(cv, ALL), pspan(m, ALL), span(cs[:, 0], ALL), ALU.mult)
                        link(V.tensor_tensor(cg[:, :], cg[:, :], cs[:, 1], ALU.mult))
                        V.tensor_tensor(qk[:, ds(i * 4 + m, 1)], cv[:, :].unsqueeze(1), cg[:, :].unsqueeze(1),
                                        ALU.add).then_inc(qk_set, 1)
                link.leave(4)
                dve.wait_ge(qk_set, 2 * HEADS + 1 + FREE)
                with dve.Fori(0, 2) as i:
                    for m in range(4):
                        dve.wait_ge(w_used, i * 4 + (U_QKV + 17 + m))
                        dve.wait_ge(v_turned, (i * 4 + (m - 1) if m >= 2 else i * 4) + FREE)
                        V.tensor_tensor(span((cg, cv)[m % 2], ALL), pspan(m % 2, ALL), span(rstd, ALL),
                                        ALU.mult).then_inc(v_norm, 1)

            def maxima(n, i, next_head=None):
                nk = sum(TILES[i + 1])
                for c in range(2):
                    dve.wait_ge(sc_ps, n * 2 + (c + 1))
                    link(V.tensor_reduce(mx[:, c:c + 1], score_row(c, P, nk), AX.X, ALU.max))
                    V.tensor_scalar(nm[:, c:c + 1], mx[:, c:c + 1], -SCALE, None, ALU.mult).then_inc(max_set, 1)
                if next_head is not None:
                    take_head(next_head)

            def take_head(h):
                V.tensor_copy(qs[:, :].unsqueeze(1), qk[:, ds(h, 1)])
                V.tensor_copy(ks[:, :].unsqueeze(1), qk[:, ds(h + HEADS, 1)]).then_inc(head_in, 1)

            def difference(n, i):
                nk = sum(TILES[i + 1])
                dve.wait_ge(probs_set, n * 2 + 2)
                if not isinstance(n, int) or n:
                    dve.wait_ge(pt_ps, n)
                link(V.reciprocal(inv[:, i], esum))
                link(V.tensor_scalar(ratio, esum[:, 0:1], inv[:, i, 1:2], nlam, ALU.mult, ALU.mult))
                V.scalar_tensor_tensor(Ab[:, 0:nk], Pb[:, 1, 0:nk], ratio, Pb[:, 0, 0:nk],
                                       ALU.mult, ALU.add).then_inc(diff_set, 1)
                dve.wait_ge(diff_set, n + 1)

            def attend(h, n, i, par, first_head=False, last=False):
                dve.wait_ge(pt_ps, n + 1)
                dve.wait_ge(o_ps, n)
                V.tensor_copy(AT[:, 1:i + 2], ps[:, 4].rearrange("p (t q) -> p t q", q=P)[:, 0:i + 1])
                V.tensor_copy(AT[0:META, 0], ps[0:META, 6, 0:P]).then_inc(at_set, 1)
                if not (last and i == NQ - 1):
                    difference(n + 1, (i + 1) % NQ)
                if not (last and i >= NQ - 2):
                    maxima(n + 2, (i + 2) % NQ, h + 1 if i == 1 and not last else None)
                if i == 2 and not first_head:
                    head_norm(h - 1, 1 - par)
                dve.wait_ge(o_ps, n + 1)
                dve.wait_ge(o_sq, n)
                V.tensor_scalar(Ob[:, par, i], ps[:, 5, P:2 * P], inv[:, i, 0:1], None, ALU.mult).then_inc(o_set, 1)
                if i == 3 and not first_head:
                    head_rest(h - 1)

            def head_norm(h, par):
                dve.wait_ge(sub_root, h + 1)
                dve.wait_ge(o_set, (h + 1) * NQ)
                dve.wait_ge(ot_ps, h + FREE)
                link(V.reciprocal(hinv, hrt))
                V.tensor_tensor(On[:, :], Ob[:, par], hinv.unsqueeze(2).broadcast_to([P, NQ, P]),
                                ALU.mult).then_inc(on_set, 1)
                dve.wait_ge(on_set, h + 1)

            def head_rest(h):
                dve.wait_ge(o_hi, h + 1)
                V.scalar_tensor_tensor(oL[:, ds(h, 1), META:L], turned_row, sub_gain,
                                       oH[:, ds(h, 1), META:L].bitcast(F32), ALU.mult, ALU.subtract).then_inc(o_lo, 1)

            def over(t, n):
                return t.unsqueeze(len(t.shape)).broadcast_to([*t.shape, n])

            def first_centred():
                dve.wait_ge(first, 1)
                s0 = ps[0:META, 4:6, 0:HEADS * META].rearrange("p c (h k) -> p c h k", k=META)
                link(V.tensor_reduce(mx0, s0, AX.X, ALU.max))
                V.tensor_tensor(S0[:, :], s0, over(mx0, META), ALU.subtract).then_inc(first, 1)

            def first_difference():
                dve.wait_ge(first, 3)
                link(V.tensor_reduce(sum0, P0[:, :], AX.X, ALU.add))
                link(V.reciprocal(inv0, sum0))
                link(V.tensor_tensor(ratio0, sum0[:, 0], inv0[:, 1], ALU.mult))
                link(V.tensor_scalar(ratio0, ratio0, nlam[0:META], None, ALU.mult))
                link(V.tensor_tensor(A0[:, :], P0[:, 1], over(ratio0, META), ALU.mult))
                V.tensor_tensor(A0[:, :], A0[:, :], P0[:, 0], ALU.add).then_inc(first, 1)

            def first_copied():
                dve.wait_ge(first, 5)
                V.tensor_copy(AT0[:, :], ps[0:META, 5, 0:HEADS * META]
                              .rearrange("p (h q) -> p h q", q=META)).then_inc(first, 1)

            def first_squares():
                dve.wait_ge(first, 7)
                o = ps[0:META, 6:8].rearrange("p a (h c) -> p (a h) c", c=P)
                link(V.tensor_tensor(O0[:, :], o, over(inv0[:, 0], P), ALU.mult))
                link(V.tensor_tensor(ON0[:, :], O0[:, :], O0[:, :], ALU.mult))
                V.tensor_reduce(sq0, ON0[:, :], AX.X, ALU.add).then_inc(first, 1)

            def first_norm():
                dve.wait_ge(first, 9)
                link(V.reciprocal(rinv0, rt0))
                V.tensor_tensor(ON0[:, :], O0[:, :], over(rinv0, P), ALU.mult).then_inc(first, 1)

            def first_rest():
                dve.wait_ge(first, 12)
                V.scalar_tensor_tensor(oL[:, :, 0:META], first_row, sub_gain, oH[:, :, 0:META].bitcast(F32),
                                       ALU.mult, ALU.subtract).then_inc(first, 1)

            def attention():
                dve.wait_ge(lam_exp, 1)
                link(V.tensor_tensor(nlam, lam_e[:, 1:2], lam_e[:, 0:1], ALU.subtract))
                link(V.tensor_scalar(nlam, nlam, LAMBDA_INIT, None, ALU.subtract))
                link(V.tensor_scalar(sub_gain, PV[:, SUBLN:SUBLN + 1], 1.0 - LAMBDA_INIT, None, ALU.mult))
                take_head(0)
                dve.wait_ge(w_used, U_WO)
                first_centred()
                maxima(0, 0)
                first_difference()
                difference(0, 0)
                maxima(1, 1)
                first_copied()
                first_squares()
                for i in range(NQ):
                    attend(0, i, i, 0, first_head=True)
                    if i == 0:
                        first_norm()
                    if i == 3:
                        first_rest()
                with dve.Fori(0, HEADS // 2 - 1) as h:
                    link.enter(h, 2 * (4 * NQ + 1))
                    for i in range(2 * NQ):
                        attend(h * 2 + (1 + i // NQ), h * (2 * NQ) + (NQ + i), i % NQ, 1 - i // NQ)
                link.leave(HEADS // 2 - 1)
                for i in range(NQ):
                    attend(HEADS - 1, (HEADS - 1) * NQ + i, i, 1, last=True)
                head_norm(HEADS - 1, 1)
                head_rest(HEADS - 1)

            def out_projection():
                with dve.Fori(0, 2) as i:
                    for m in range(4):
                        n = i * 4 + m
                        dve.wait_ge(w_used, n + (U_WO + 1))
                        V.tensor_tensor(span(hT[:, ds(n, 1)].rearrange("p a t -> p (a t)"), ALL),
                                        span(hT[:, ds(n, 1)].rearrange("p a t -> p (a t)"), ALL),
                                        pspan(m % 2, ALL), ALU.add).then_inc(h_new[2], 1)
                        split_gain(2, n, i * 4 + (GAIN_FFN + 8 + m), n + 1)

            def add_down(l, ct, used, m, spans):
                dve.wait_ge(w_used, used)
                h = span(hT[:, ds(ct, 1)].rearrange("p a t -> p (a t)"), spans)
                V.tensor_tensor(h, h, pspan(2 + m % 2, spans), ALU.add).then_inc(h_new[1 + 2 * l], 1)

            glu()
            ffn(0, ALL, ALL, 0)
            dve.wait_ge(lam_in, 16)
            t = tiny[:, 384:512].rearrange("p (a b) -> p a b", a=2)
            l4 = lam.rearrange("p (a c b) -> p a c b", a=2, c=2)
            link(V.tensor_tensor(t, l4[:, :, 0], l4[:, :, 1], ALU.mult))
            V.tensor_reduce(lam_s, t, AX.X, ALU.add).then_inc(lam_sum, 1)
            qkv()
            attention()
            out_projection()
            ffn(1, FROM12, FROM16, META)

        @block.gpsimd
        def _(pool):
            V = nc.gpsimd
            link = Chain(pool, pool_seq)

            def cmul(o, a, b, t):
                V.tensor_tensor(t[0], a[0], b[0], ALU.mult)
                V.tensor_tensor(t[1], a[1], b[1], ALU.mult)
                V.tensor_tensor(t[2], a[1], b[0], ALU.mult)
                link(V.tensor_tensor(t[3], a[0], b[1], ALU.mult))
                V.tensor_tensor(o[0], t[0], t[1], ALU.subtract)
                link(V.tensor_tensor(o[1], t[2], t[3], ALU.add))

            tp = [tmpP[:, k * 256:(k + 1) * 256] for k in range(4)]
            pool.wait_ge(w_phasor, 1)
            src = sm[:, 5:7]
            for k in range(9):
                sq = tp[0][:, 0:2 * G].rearrange("p (a g) -> p a g", a=2)
                V.tensor_tensor(sq, src, src, ALU.mult)
                link(V.tensor_tensor(tp[1][:, 0:G], src[:, 0], src[:, 1], ALU.mult))
                V.tensor_tensor(pw[:, 2 * k], sq[:, 0], sq[:, 1], ALU.subtract)
                ins = V.tensor_tensor(pw[:, 2 * k + 1], tp[1][:, 0:G], tp[1][:, 0:G], ALU.add)
                if k < 8:
                    link(ins)
                src = pw[:, 2 * k:2 * k + 2]
            ins.then_inc(pw_set, 1)
            V.memset(TA1[:, :, 0:1], 1.0)
            link(V.memset(TA2[:, :, 0:1], 0.0))
            power_table(cmul, TA1, TA2, 8, 8, tp)
            V.memset(tp[0][:, 0:1], 0.0).then_inc(ta_set, 1)
            pool.wait_ge(ta_set, 1)

            def normed(b, par):
                pool.wait_ge(xb_in[par], (b - par) * 16 + 32)
                pool.wait_ge(u_ps, b)
                normed_x(V, b, par)

            def input_weights(b):
                pool.wait_ge(k_ps, b)
                input_powers(V, link, F, b, tmpP[:, :])
                pool.wait_ge(f_set, b + 1)

            def rotation(b, par):
                if not isinstance(b, int) or b >= 2:
                    pool.wait_ge(s_set, b - 1)
                o = T1[:, par].rearrange("p g (a b) -> p g a b", b=8)
                t = tmpP[:, 0:576].rearrange("p (g a b) -> p g a b", g=BG, b=8)
                low = lambda x: x[:, ds(b * BG, BG)].unsqueeze(2).broadcast_to([P, BG, 9, 8])
                high = lambda x: x[:, ds(b * BG, BG)].unsqueeze(3).broadcast_to([P, BG, 9, 8])
                V.tensor_tensor(o, low(TA1), high(TB1), ALU.mult)
                link(V.tensor_tensor(t, low(TA2), high(TB2), ALU.mult))
                V.tensor_tensor(o, o, t, ALU.subtract).then_inc(t1_set, 1)
                pool.wait_ge(t1_set, b + 1)

            pool.wait_ge(tb_set, 1)
            rotation(0, 0)
            pool.wait_ge(xr_set, 1)
            normed(1, 1)
            input_weights(1)
            rotation(1, 1)
            with pool.Fori(0, 3) as i:
                link.enter(i, 4)
                for par in range(2):
                    b = i * 2 + (par + 2)
                    input_weights(b)
                    normed(b, par)
                    rotation(b, par)
            link.leave(3)
            for n in range(2):
                split_lo(pool, n, n)

            def square(i, ct, n):
                pool.wait_ge(h_new[i], n + FREE)
                link(V.tensor_tensor(sqt[:, :].unsqueeze(1), hT[:, ds(ct, 1)], hT[:, ds(ct, 1)], ALU.mult))
                V.tensor_tensor(acc[:, :], acc[:, :], sqt[:, :], ALU.add).then_inc(sq_sum[i], 1)
                pool.wait_ge(sq_sum[i], n)

            def glu():
                for n in (2, 3):
                    split_lo(pool, n, n)
                pool.wait_ge(glu_free, 1 + FREE)
                with pool.Fori(0, 4) as i:
                    link.enter(i, 2)
                    for q in range(2):
                        for c in range(2):
                            split_lo(pool, i * 4 + (4 + 2 * q + c), 2 * q + c)
                        square(0, i * 2 + q, i * 2 + (q + 1))
                link.leave(4)

            def ffn(l):
                nu, nd = (U_UP0, U_DN0) if l == 0 else (U_UP1, U_DN1)
                if l == 0:
                    clear_sum(0)
                with pool.Fori(0, FT // 2) as i:
                    for c in range(4):
                        split_lo(pool, i * 4 + (nu + 4 + c), c)
                if l == 0:
                    with pool.Fori(0, 2) as i:
                        link.enter(i, 4)
                        for m in range(4):
                            for kc in range(3):
                                c = 3 * m + kc
                                split_lo(pool, i * 12 + (nd + 4 + c), c % 4, (8, 8, 6)[(c + 4) % 3] if c < 8 else 8)
                            square(1, i * 4 + m, i * 4 + (m + 1))
                    link.leave(2)

                if l == 1:
                    for c in range(20):
                        split_lo(pool, nd + 4 + c, c % 4, (8, 8, 6)[(c + 4) % 3])

            def clear_sum(i):
                pool.wait_ge(stat_ps[i], 1)
                link(V.memset(acc[:, :], 0.0))

            def qkv():
                clear_sum(1)
                with pool.Fori(0, 6) as i:
                    for c in range(4):
                        split_lo(pool, i * 4 + (U_QKV + 4 + c), c)

            def out_projection():
                with pool.Fori(0, 2) as i:
                    link.enter(i, 4)
                    for m in range(4):
                        split_lo(pool, i * 4 + (U_WO + 4 + m), m)
                        square(2, i * 4 + m, i * 4 + (m + 1))
                link.leave(2)

            glu()
            ffn(0)
            qkv()
            out_projection()
            ffn(1)


_INS = ["x", "meta_tokens", "norm_mix_gain", "norm_ffn_gain", "s5_a_re", "s5_a_im", "s5_log_dt", "s5_b_re", "s5_b_im",
        "s5_c_re", "s5_c_im", "s5_d", "s5_w_glu", "s5_b_glu", "attn_w_qkv", "attn_lambda", "attn_subln_gain",
        "attn_w_o", "ffn_w_up", "ffn_conv_w", "ffn_conv_b", "ffn_w_down", "final_norm_gain"]


def kernel(**inputs):
    import concourse.bacc as bacc
    from concourse.bass_utils import run_bass_kernel_spmd

    nc = bacc.Bacc("TRN2", target_bir_lowering=False, num_devices=1)
    arrays = {n: np.ascontiguousarray(inputs[n]) for n in _INS}
    aps = {n: nc.dram_tensor(n, a.shape, mybir.dt.from_np(a.dtype), kind="ExternalInput").ap()
           for n, a in arrays.items()}
    out = nc.dram_tensor("out", (1, SEQ, D), F32, kind="ExternalOutput").ap()
    build(nc, aps, out)
    r = run_bass_kernel_spmd(nc, [arrays], core_ids=[0])
    return r.results[0]["out"]
```
